# Optimizing a Trainium2 kernel written in Bass

```python
import jax, jax.numpy as jnp
from jax import lax
import numpy as np

D_MODEL = 1024
BATCH = 1
SEQ = 1024
DEPTH = 1
DEC_BATCH = 8
DEC_SEQ = 4
PAST_LEN = 4096
PAGE_SIZE = 128

C_CONV = D_MODEL
CONV_WIDTH = 31
N_HEADS = 8
QK_NOPE = 128
QK_ROPE = 64
V_DIM = 128
Q_LORA = 384
KV_LORA = 256
ROPE_THETA = 10000.0
Q_BLOCK = 128
ATTN_SCALE = (QK_NOPE + QK_ROPE) ** -0.5
D_FF = 2816
FFN_CONV_WIDTH = 3
DN_ALPHA = (2.0 * DEPTH) ** 0.25
DN_BETA = (8.0 * DEPTH) ** -0.25
LN_EPS = 1e-5
RMS_EPS = 1e-6
SPLIT_Q = 2 * C_CONV
SPLIT_KV = SPLIT_Q + Q_LORA
SPLIT_KR = SPLIT_KV + KV_LORA
SPLIT_GATE = SPLIT_KR + QK_ROPE
IN_WIDTH = SPLIT_GATE + 2 * D_MODEL
POOL_NUM, POOL_DEN = 5, 4

kernel_name = 'hybrid_conformer_mla_convffn_deepnorm_step'

def _layer_norm(x, g, b):
    xf = x.astype(jnp.float32)
    mu = jnp.mean(xf, axis=-1, keepdims=True)
    var = jnp.mean(jnp.square(xf - mu), axis=-1, keepdims=True)
    return ((xf - mu) * lax.rsqrt(var + LN_EPS)).astype(x.dtype) * g + b

def _rms_norm(x, g):
    xf = x.astype(jnp.float32)
    ms = jnp.mean(jnp.square(xf), axis=-1, keepdims=True)
    return (xf * lax.rsqrt(ms + RMS_EPS)).astype(x.dtype) * g

def _causal_dwconv(prev, u, w, b):
    ext = jnp.concatenate([prev.astype(u.dtype), u], axis=1)
    y = lax.conv_general_dilated(ext, w[:, None, :].astype(u.dtype), window_strides=(1,), padding='VALID',
                                 dimension_numbers=('NWC', 'WIO', 'NWC'), feature_group_count=u.shape[-1])
    return y + b, ext[:, -(w.shape[0] - 1):]

def _rope_tables(positions):
    inv = 1.0 / (ROPE_THETA ** (jnp.arange(0, QK_ROPE, 2, dtype=jnp.float32) / QK_ROPE))
    ang = positions.astype(jnp.float32)[:, None] * inv[None, :]
    return jnp.cos(ang), jnp.sin(ang)

def _apply_rope(x, cos, sin):
    x1, x2 = jnp.split(x, 2, axis=-1)
    cos = cos.astype(x.dtype)
    sin = sin.astype(x.dtype)
    return jnp.concatenate([x1 * cos - x2 * sin, x1 * sin + x2 * cos], axis=-1)

def _prompt_attention(q_lat, q_rope, c_kv, k_rope):
    B, S = q_lat.shape[:2]
    nb = S // Q_BLOCK
    ql = jnp.moveaxis(q_lat.reshape(B, nb, Q_BLOCK, N_HEADS, KV_LORA), 1, 0)
    qr = jnp.moveaxis(q_rope.reshape(B, nb, Q_BLOCK, N_HEADS, QK_ROPE), 1, 0)
    k_pos = jnp.arange(S)

    def block(args):
        i, ql_b, qr_b = args
        s = jnp.einsum('bqhl,bkl->bhqk', ql_b, c_kv) + jnp.einsum('bqhr,bkr->bhqk', qr_b, k_rope)
        s = s.astype(jnp.float32) * ATTN_SCALE
        q_pos = i * Q_BLOCK + jnp.arange(Q_BLOCK)
        s = jnp.where(q_pos[:, None] >= k_pos[None, :], s, -jnp.inf)
        p = jax.nn.softmax(s, axis=-1).astype(c_kv.dtype)
        return jnp.einsum('bhqk,bkl->bqhl', p, c_kv)

    o = lax.map(block, (jnp.arange(nb), ql, qr))
    return jnp.moveaxis(o, 0, 1).reshape(B, S, N_HEADS, KV_LORA)

def _make_sample_attention(pool_c, pool_kr, page_table):
    def attend(q_lat, q_rope, c_new, kr_new):
        T = q_lat.shape[1]
        causal = jnp.tril(jnp.ones((T, T), dtype=bool))

        def one(args):
            ql, qr, cn, krn, pages = args
            c_past = pool_c[pages].reshape(-1, KV_LORA).astype(cn.dtype)
            kr_past = pool_kr[pages].reshape(-1, QK_ROPE).astype(cn.dtype)
            s_past = jnp.einsum('thl,kl->htk', ql, c_past) + jnp.einsum('thr,kr->htk', qr, kr_past)
            s_new = jnp.einsum('thl,sl->hts', ql, cn) + jnp.einsum('thr,sr->hts', qr, krn)
            s_past = s_past.astype(jnp.float32) * ATTN_SCALE
            s_new = jnp.where(causal, s_new.astype(jnp.float32) * ATTN_SCALE, -jnp.inf)
            p = jax.nn.softmax(jnp.concatenate([s_past, s_new], axis=-1), axis=-1).astype(cn.dtype)
            n_past = c_past.shape[0]
            return (jnp.einsum('htk,kl->thl', p[..., :n_past], c_past)
                    + jnp.einsum('hts,sl->thl', p[..., n_past:], cn))

        return lax.map(one, (q_lat, q_rope, c_new, kr_new, page_table))
    return attend

def _layer(x, positions, conv_prev, ffn_prev, attend, p):
    B, T, _ = x.shape
    z = x @ p['w_in'] + p['b_in']
    z_glu, z_q, z_kv, z_kr, z_gate = jnp.split(z, [SPLIT_Q, SPLIT_KV, SPLIT_KR, SPLIT_GATE], axis=-1)
    a, g = jnp.split(z_glu, 2, axis=-1)
    u, conv_state = _causal_dwconv(conv_prev, a * jax.nn.sigmoid(g), p['conv_dw_w'], p['conv_dw_b'])
    y_conv = jax.nn.silu(_layer_norm(u, p['conv_ln_g'], p['conv_ln_b'])) @ p['w_conv_out']
    cos, sin = _rope_tables(positions)
    q = (_rms_norm(z_q, p['q_norm_g']) @ p['w_uq']).reshape(B, T, N_HEADS, QK_NOPE + QK_ROPE)
    q_nope = q[..., :QK_NOPE]
    q_rope = _apply_rope(q[..., QK_NOPE:], cos[:, None, :], sin[:, None, :])
    q_lat = jnp.einsum('bthn,lhn->bthl', q_nope, p['w_uk'])
    c_kv = _rms_norm(z_kv, p['kv_norm_g'])
    k_rope = _apply_rope(z_kr, cos, sin)
    o_lat = attend(q_lat, q_rope, c_kv, k_rope)
    v = jnp.einsum('bthl,lhv->bthv', o_lat, p['w_uv']).reshape(B, T, N_HEADS * V_DIM)
    y_mla = v @ p['w_mla_out']
    g_conv, g_mla = jnp.split(jax.nn.sigmoid(z_gate), 2, axis=-1)
    mix = (g_conv * y_conv + g_mla * y_mla) @ p['w_mix_out']
    x1 = _layer_norm(DN_ALPHA * x + mix, p['ln1_g'], p['ln1_b'])
    h, ffn_state = _causal_dwconv(ffn_prev, x1 @ p['w_up'], p['ffn_dw_w'], p['ffn_dw_b'])
    hg, hv = jnp.split(h, 2, axis=-1)
    f = (jax.nn.silu(hg) * hv) @ p['w_down']
    y = _layer_norm(DN_ALPHA * x1 + f, p['ln2_g'], p['ln2_b'])
    return y, c_kv, k_rope, conv_state, ffn_state

def setup_inputs(seed: int = 0) -> dict:
    key = jax.random.key(seed)
    ks = jax.random.split(key, 40)
    n_pages = PAST_LEN // PAGE_SIZE
    n_pool = (DEC_BATCH * n_pages * POOL_NUM) // POOL_DEN

    def w(k, shape, fan_in, scale=1.0):
        return jax.random.normal(k, (DEPTH,) + shape, jnp.float32) * (fan_in ** -0.5) * scale

    def gain(k, shape):
        return 1.0 + 0.05 * jax.random.normal(k, (DEPTH,) + shape, jnp.float32)

    def bias(k, shape):
        return 0.02 * jax.random.normal(k, (DEPTH,) + shape, jnp.float32)

    page_table = jax.random.permutation(ks[0], n_pool)[:DEC_BATCH * n_pages].reshape(DEC_BATCH, n_pages).astype(jnp.int32)
    return {
        'x_prompt': jax.random.normal(ks[1], (BATCH, SEQ, D_MODEL), jnp.float32),
        'x_sample': jax.random.normal(ks[2], (DEC_BATCH, DEC_SEQ, D_MODEL), jnp.float32),
        'cache_kv_latent': jax.random.normal(ks[3], (DEPTH, n_pool, PAGE_SIZE, KV_LORA), jnp.float32),
        'cache_k_rope': jax.random.normal(ks[4], (DEPTH, n_pool, PAGE_SIZE, QK_ROPE), jnp.float32),
        'state_conv': jax.random.normal(ks[5], (DEPTH, DEC_BATCH, CONV_WIDTH - 1, C_CONV), jnp.float32),
        'state_ffn_conv': jax.random.normal(ks[6], (DEPTH, DEC_BATCH, FFN_CONV_WIDTH - 1, 2 * D_FF), jnp.float32),
        'page_table': page_table,
        'w_in': w(ks[7], (D_MODEL, IN_WIDTH), D_MODEL),
        'b_in': bias(ks[8], (IN_WIDTH,)),
        'conv_dw_w': w(ks[9], (CONV_WIDTH, C_CONV), CONV_WIDTH),
        'conv_dw_b': bias(ks[10], (C_CONV,)),
        'conv_ln_g': gain(ks[11], (C_CONV,)),
        'conv_ln_b': bias(ks[12], (C_CONV,)),
        'w_conv_out': w(ks[13], (C_CONV, D_MODEL), C_CONV),
        'q_norm_g': gain(ks[14], (Q_LORA,)),
        'w_uq': w(ks[15], (Q_LORA, N_HEADS * (QK_NOPE + QK_ROPE)), Q_LORA),
        'kv_norm_g': gain(ks[16], (KV_LORA,)),
        'w_uk': w(ks[17], (KV_LORA, N_HEADS, QK_NOPE), KV_LORA),
        'w_uv': w(ks[18], (KV_LORA, N_HEADS, V_DIM), KV_LORA, DN_BETA),
        'w_mla_out': w(ks[19], (N_HEADS * V_DIM, D_MODEL), N_HEADS * V_DIM),
        'w_mix_out': w(ks[20], (D_MODEL, D_MODEL), D_MODEL, DN_BETA),
        'ln1_g': gain(ks[21], (D_MODEL,)),
        'ln1_b': bias(ks[22], (D_MODEL,)),
        'w_up': w(ks[23], (D_MODEL, 2 * D_FF), D_MODEL),
        'ffn_dw_w': w(ks[24], (FFN_CONV_WIDTH, 2 * D_FF), FFN_CONV_WIDTH),
        'ffn_dw_b': bias(ks[25], (2 * D_FF,)),
        'w_down': w(ks[26], (D_FF, D_MODEL), D_FF, DN_BETA),
        'ln2_g': gain(ks[27], (D_MODEL,)),
        'ln2_b': bias(ks[28], (D_MODEL,)),
    }

def reference(x_prompt, x_sample, cache_kv_latent, cache_k_rope, state_conv, state_ffn_conv, page_table,
              w_in, b_in, conv_dw_w, conv_dw_b, conv_ln_g, conv_ln_b, w_conv_out, q_norm_g, w_uq, kv_norm_g,
              w_uk, w_uv, w_mla_out, w_mix_out, ln1_g, ln1_b, w_up, ffn_dw_w, ffn_dw_b, w_down, ln2_g, ln2_b):
    B, S, _ = x_prompt.shape
    T = x_sample.shape[1]
    n_pages = page_table.shape[1]
    past_len = n_pages * PAGE_SIZE
    pos_prompt = jnp.arange(S, dtype=jnp.int32)
    pos_sample = past_len + jnp.arange(T, dtype=jnp.int32)
    h_p, h_s = x_prompt, x_sample
    c_p, kr_p, cv_p, ff_p = [], [], [], []
    c_s, kr_s, cv_s, ff_s = [], [], [], []
    for l in range(DEPTH):
        p = dict(w_in=w_in[l], b_in=b_in[l], conv_dw_w=conv_dw_w[l], conv_dw_b=conv_dw_b[l],
                 conv_ln_g=conv_ln_g[l], conv_ln_b=conv_ln_b[l], w_conv_out=w_conv_out[l],
                 q_norm_g=q_norm_g[l], w_uq=w_uq[l], kv_norm_g=kv_norm_g[l], w_uk=w_uk[l], w_uv=w_uv[l],
                 w_mla_out=w_mla_out[l], w_mix_out=w_mix_out[l], ln1_g=ln1_g[l], ln1_b=ln1_b[l],
                 w_up=w_up[l], ffn_dw_w=ffn_dw_w[l], ffn_dw_b=ffn_dw_b[l], w_down=w_down[l],
                 ln2_g=ln2_g[l], ln2_b=ln2_b[l])
        conv0 = jnp.zeros((B, CONV_WIDTH - 1, C_CONV), h_p.dtype)
        ffn0 = jnp.zeros((B, FFN_CONV_WIDTH - 1, 2 * D_FF), h_p.dtype)
        h_p, ckv, kr, cst, fst = _layer(h_p, pos_prompt, conv0, ffn0, _prompt_attention, p)
        c_p.append(ckv); kr_p.append(kr); cv_p.append(cst); ff_p.append(fst)
        attend = _make_sample_attention(cache_kv_latent[l], cache_k_rope[l], page_table)
        h_s, ckv, kr, cst, fst = _layer(h_s, pos_sample, state_conv[l], state_ffn_conv[l], attend, p)
        c_s.append(ckv); kr_s.append(kr); cv_s.append(cst); ff_s.append(fst)
    return (h_p, h_s,
            jnp.stack(c_p, 0), jnp.stack(kr_p, 0), jnp.stack(cv_p, 0), jnp.stack(ff_p, 0),
            jnp.stack(c_s, 0), jnp.stack(kr_s, 0), jnp.stack(cv_s, 0), jnp.stack(ff_s, 0))


_drawn_inputs = setup_inputs


def setup_inputs(seed=0):
    import zlib

    import numpy as np

    out = dict(_drawn_inputs(seed))
    spreads = {}
    factors = {'cache_kv_latent': 8.0,
     'cache_k_rope': 8.0,
     'b_in': 2.688,
     'conv_dw_b': 8.0,
     'conv_ln_g': 5.674,
     'conv_ln_b': 21.554,
     'q_norm_g': 8.0,
     'w_uq': 3.289,
     'w_uk': 3.587,
     'ln1_b': 2.73,
     'ffn_dw_b': 6.649,
     'ln2_b': 2.741}
    for name, (base, spread) in spreads.items():
        noise = np.random.default_rng([zlib.crc32(name.encode()), seed]).standard_normal(out[name].shape)
        drawn = base * np.exp(spread * noise) if base else spread * noise
        out[name] = __import__('jax').numpy.asarray(drawn.astype(out[name].dtype))
    for name, factor in factors.items():
        out[name] = (out[name] * factor).astype(out[name].dtype)
    return out
```

```python
from contextlib import ExitStack

import numpy as np

import concourse.bass as bass
from concourse import mybir

F32 = mybir.dt.float32
F32R = mybir.dt.float32r
BF16 = mybir.dt.bfloat16
I32 = mybir.dt.int32
ALU = mybir.AluOpType
ACT = mybir.ActivationFunctionType
AX = mybir.AxisListType

P = 128
D = 1024
S = 1024
NB, NT = 8, 4
NS = NB * NT
T = S + NS
CW = 31
FW = 3
H = 8
DN, DR, DV = 128, 64, 128
QL, KL = 384, 256
PAST, PAGE = 4096, 128
NPAGES = PAST // PAGE
F = 2816
SCALE = (DN + DR) ** -0.5
ALPHA = 2.0 ** 0.25
LN_EPS, RMS_EPS = 1e-5, 1e-6
C_Q = 2 * D
C_KV = C_Q + QL
C_KR = C_KV + KL
C_G = C_KR + DR
NEG = -1.0e30

MT = D // P
CH = T // 3
KT = D // P
FT = F // P
HALO = CW - 1
KEEP = HALO + NS

V_A, V_GL, V_Q, V_KV, V_KR = 0, 8, 16, 19, 21
V_GA, V_GB, V_CB, V_LG, V_LB, V_QG, V_KG, V_FB = 22, 30, 38, 46, 54, 62, 65, 67
V_L1G = V_FB + 2 * FT
V_L1B = V_L1G + MT
V_ROWS = V_L1B + MT


def program(nc, A, O):
    ctx = ExitStack()
    with ctx:
        base0 = (nc.sbuf_base + 63) // 64 * 64
        top = nc.sbuf_usable_end

        def at(name, shape, dt, off):
            size = int(np.prod(shape[1:])) * (2 if dt == BF16 else 4)
            assert base0 + off + size <= top, (name, base0 + off + size, top)
            return nc.alloc_sbuf_tensor_at(name, shape, dt, offset=base0 + off)

        def sem(name):
            return ctx.enter_context(nc.semaphore(name))

        ident = at("ident", [P, P], F32, 0)
        maskc = at("maskc", [P, P], F32, 512)
        ones = at("ones", [P, P], F32, 1024)
        vec = at("vec", [P, V_ROWS + 1], F32, 1536)
        cwv = at("cwv", [P, CW * MT], F32, 2048)
        fwv = at("fwv", [P, FW * 2 * FT], F32, 3072)
        maskb = at("maskb", [P, P], BF16, 3648)
        identb = at("identb", [P, P], BF16, 3904)
        wtap = at("wtap", [P, 2, CW + 1], F32, 4160)
        RAW, HL = 2, 4
        R0 = 4480
        wraw = at("wraw", [P, RAW, D], F32, R0)
        whi = at("whi", [P, HL, D], F32R, R0 + 8192)
        wlo = at("wlo", [P, HL, D], F32R, R0 + 24576)
        R1 = R0 + 40960
        XB = MT * T * 4
        xh = at("xh", [P, MT, T], F32R, R1)
        xl = at("xl", [P, MT, T], F32R, R1 + XB)
        u = at("u", [P, MT, T], F32, R1 + 2 * XB)
        sl = at("sl", [P, MT, T], F32R, R1 + 2 * XB)
        sh = at("sh", [P, MT, T], F32R, R1 + 3 * XB)
        Y = R1 + 3 * XB
        GB = 4352
        g_ext = [at(f"g_ext{j}", [P, HALO + T], F32, Y + j * GB) for j in range(2)]
        gs_ext = [at(f"gs_ext{j}", [P, NB, HALO + NT], F32, Y + 2 * GB + j * 1088) for j in range(2)]
        stT = at("stT", [P, MT, NB * HALO], F32, Y + 2 * GB + 2176)
        keep = at("keep", [P, MT, KEEP], F32, Y + 2 * GB + 2176 + 7680)
        sg = [at(f"sg{j}", [P, T], F32, Y + 2 * GB + 2176 + 7680 + 1984 + j * T * 4) for j in range(2)]
        strows = at("strows", [NB * HALO // 2, 2, D], F32, Y + 2 * GB + 2176 + 7680 + 1984)
        Z = R1 + 4 * XB
        stat = at("stat", [P, T], F32, Z)
        s1 = at("s1", [P, T], F32, Z + 4224)
        tmp = [at(f"tmp{j}", [P, T], F32, Z + 8448 + j * 4224) for j in range(2)]
        krow = [at(f"krow{j}", [32, D], F32, Z + 8448 + j * 4224) for j in range(2)]
        stg = [at(f"stg{j}", [P, T], F32, Z + 16896 + j * 4224) for j in range(2)]
        xrow = [at(f"xrow{j}", [P, D], F32, R1 + 2 * XB + j * 4096) for j in range(4)]
        xst = [at(f"xst{j}", [P, MT, P], F32, R1 + 2 * XB + 16384 + j * 4096) for j in range(2)]
        vrow = at("vrow", [P, P], F32, R1 + 2 * XB + 24576)
        crow = at("crow", [P, 2, P], F32, R1 + 2 * XB + 25088)
        frow = at("frow", [P, 2, P], F32, R1 + 2 * XB + 26112)

        psx = [ctx.enter_context(nc.psum_tensor(f"ps{n}", [P, 3, 512], F32)) for n in "ab"]
        pst = ctx.enter_context(nc.psum_tensor("pst", [P, 2, 512], F32))

        def acc(j):
            return psx[j % 2][:, :, 0:CH]

        def dram(name, shape):
            return nc.dram_tensor(name, shape, F32, kind="Internal").ap()

        xt_d = dram("xt_d", [MT, P, T])
        ga_d = dram("ga_d", [MT, P, T])
        gb_d = dram("gb_d", [MT, P, T])
        z_d = dram("z_d", [6, P, T])
        ma_d = dram("ma_d", [MT, P, T])

        X0 = R1
        zbuf = at("zbuf", [P, 6, T], F32, X0)
        qnl = at("qnl", [P, 3, T], F32R, X0 + 3 * 4224)
        gab = [at(f"gab{j}", [P, T], F32, X0 + 25344 + j * 4224) for j in range(2)]
        sqb = at("sqb", [P, 5, T], F32, X0 + 33792)
        ckvh = at("ckvh", [P, 2, T], F32R, X0 + 33792)
        ckvl = at("ckvl", [P, 2, T], F32R, X0 + 42240)
        kr2 = at("kr2", [P, T], F32R, X0 + 50688)
        krl = at("krl", [P, T], F32R, X0 + 54912)
        cs = at("cs", [P, T], F32, X0 + 59136)
        rk = at("rk", [P, T], F32, X0 + 63360)
        qnh = at("qnh", [P, 3, T], F32R, Z)
        rq = at("rq", [P, T], F32, Z + 12672)
        qrt2 = at("qrt2", [P, T], F32, X0 + 54912)



        U0 = X0 + 2 * XB
        orow = [at(f"orow{j}", [P, KL + DR], F32, X0 + 25344 + j * 1280) for j in range(2)]
        qh = at("qh", [P, T], F32R, X0)
        ql = at("ql", [P, T], F32R, X0 + 4224)
        qr2 = at("qr2", [P, T], F32R, X0 + 8448)
        qrt = at("qrt", [P, T], F32, X0 + 8448)
        qrf = at("qrf", [P, T], F32, X0 + 63360)
        vt = at("vt", [P, H, T], F32, U0)
        pth = at("pth", [P, 8, 2 * P], F32R, U0 + 33792)
        ptl = at("ptl", [P, 8, 2 * P], F32R, U0 + 41984)
        knh = at("knh", [P, S], F32R, U0 + 50176)
        knl = at("knl", [P, S], F32R, U0 + 54272)
        vh = at("vh", [P, 8, P], F32R, U0 + 58368)
        vl = at("vl", [P, 8, P], F32R, U0 + 62464)
        pbuf = [at(f"pbuf{j}", [P, S], F32, Z + 16896 + j * 4096) for j in range(2)]
        qsn = at("qsn", [P, H, NS], F32, Z + 25088)
        qsr = at("qsr", [P, H, NS], F32, Z + 26112)
        cnr = at("cnr", [NS, KL], F32, Z + 27136)
        mnew = at("mnew", [NS, NB, H * NT], F32, Z + 28160)
        cnT = at("cnT", [P, 2, NS], F32, Z + 29184)
        krT = at("krT", [DR, NS], F32, Z + 29440)
        idx = at("idx", [P, NB, 5], I32, Z + 29568)
        ptb = at("ptb", [P, NB], I32, Z + 29728)
        part = at("part", [P, 5], F32, Z + 29760)
        nmx = at("nmx", [P, 8], F32, Z + 29792)
        rs = at("rs", [P, 8], F32, Z + 29824)
        rr = at("rr", [P, 8], F32, Z + 29856)
        HT = H * NT
        NTL = PAST // P
        cb = [at(f"cb{j}", [P, NTL, KL], F32, X0 + j * 32768) for j in range(2)]
        kb = [at(f"kb{j}", [P, NTL, DR], F32, Z + j * 8192) for j in range(2)]
        wukp = at("wukp", [P, 2, H * DN], F32, X0 + 32768)
        wukT = at("wukT", [P, H, 2, P], F32, Z + 16384)
        ol = at("ol", [P, 2, NB, HT], F32, X0 + 65536)
        ct = [at(f"ct{j}", [P, 8, P], F32, U0 + 33792 + j * 4096) for j in range(2)]
        rt = at("rt", [P, 4, P], F32, U0 + 41984)
        px = [at(f"px{j}", [P, NTL, HT], F32, U0 + 44032 + j * 4096) for j in range(2)]
        wuvp = at("wuvp", [P, 2, H * DV], F32, U0 + 52224)
        qall = at("qall", [P, 4, NB, HT], F32, U0 + 60416)
        qcur = [at(f"qcur{j}", [P, 4, HT], F32, U0 + 64512 + j * 512) for j in range(2)]
        m1 = at("m1", [P, HT], F32, U0 + 65536)
        bcs = at("bcs", [P, HT], F32, U0 + 65664)
        rs1 = at("rs1", [P, HT], F32, U0 + 65792)
        rb = at("rb", [P, HT], F32, U0 + 65920)
        dg = at("dg", [HT, HT], F32, U0 + 66048)
        sn = at("sn", [NS, HT], F32, U0 + 66176)
        mxr = at("mxr", [HT, 1], F32, U0 + 66304)
        vth = at("vth", [P, MT, T], F32R, X0)
        vtl = at("vtl", [P, MT, T], F32R, X0 + XB)
        mgh = at("mgh", [P, MT, T], F32R, U0)
        mgl = at("mgl", [P, MT, T], F32R, X0 + 3 * XB)
        mt = (stat, s1)
        res = at("res", [P, MT, T], F32, X0)
        frows = at("frows", [NB * (FW - 1), 2 * F], F32, X0 + XB)
        pfx = at("pfx", [P, 2 * FT, NB, FW - 1], F32, Z + 25344)
        x1h = at("x1h", [P, MT, T], F32R, X0 + XB)
        x1l = at("x1l", [P, MT, T], F32R, U0)
        fh = [at(f"fh{j}", [P, 2, T], F32R, X0 + 3 * XB + j * 8448) for j in range(2)]
        fl = [at(f"fl{j}", [P, 2, T], F32R, X0 + 3 * XB + 16896 + j * 8448) for j in range(2)]
        ue = [at(f"ue{n}", [P, FW - 1 + T], F32, Z + j * 4256) for j, n in enumerate("gv")]
        hb = [at(f"h{n}", [P, T], F32, Z + 8512 + j * 4224) for j, n in enumerate("gv")]
        se = [at(f"se{n}", [P, NB, FW - 1 + NT], F32, Z + 16960 + j * 192) for j, n in enumerate("gv")]
        FK = (FW - 1) * (1 + NB)
        kf = at("kf", [P, 2 * FT, FK], F32, Z + 17344)
        yrow = [at(f"yrow{j}", [P, D], F32, X0 + XB + j * 4096) for j in range(4)]
        fout = at("fout", [FK, 2 * F], F32, U0)
        g2 = at("g2", [P, D], F32, Z)
        b2 = at("b2", [P, D], F32, Z + 4256)
        bst = [at(f"bst{j}", [P, 2, 6], F32, Z + 20544 + j * 64) for j in range(2)]
        mv = [at(f"mv{j}", [P, 2], F32, Z + 20672 + j * 32) for j in range(2)]
        sd = [at(f"sd{j}", [P, 2], F32, Z + 20736 + j * 32) for j in range(2)]

        c_in = sem("consts_in")
        c2_in = sem("mask_in")
        cs_in = sem("rope_table_in")
        v_in = sem("vector_rows_in")
        st_in = sem("state_rows_in")
        x_in = [sem(f"x_rows_in{j}") for j in range(4)]
        ones_set = sem("ones_set")
        halo_set = sem("halo_zeroed")
        tr_done = sem("start_transposed")
        tr_read = sem("start_transposes_read")
        xt_ready = sem("x_tile_in_psum")
        x_hi = sem("x_hi_done")
        xt_out = [sem(f"xt_out{j}") for j in range(2)]
        raw_in = [sem(f"w_raw_in{j}") for j in range(RAW)]
        kr_in = sem("w_kr_in")
        hi_done = sem("w_hi_done")
        lo_done = sem("w_lo_done")
        w_used = sem("w_used")
        free = [sem(f"acc_read_{n}") for n in "ab"]
        st_copied = sem("state_prefix_copied")
        conv_chain = sem("conv_chain")
        conv_done = sem("conv_done")
        stg_out = [sem(f"stage_out{j}") for j in range(2)]
        keep_tr = sem("keep_transposed")
        keep_rd = sem("keep_rows_read")
        out_s = sem("outputs_written")
        krow_out = sem("conv_state_rows_out")
        stat_done = sem("column_sums_done")
        ln_c = sem("conv_centred")
        ln_sq = sem("conv_squared")
        ln_s2 = sem("conv_squares_added")
        rstd_done = sem("rstd_done")
        ln_n = sem("conv_normalised")
        ln_act = sem("conv_swish_done")
        sh_done = sem("swish_hi_done")
        sl_done = sem("swish_lo_done")
        ga_in = [sem(f"gate_a_in{j}") for j in range(2)]
        ma_out = [sem(f"merged_a_out{j}") for j in range(2)]
        z_in = sem("z_reloaded")
        rms_sq = sem("rms_squared")
        rms_n = sem("rms_scaled")
        rms_h = sem("rms_hi_done")
        rms_l = sem("rms_lo_done")
        rms_c = sem("rms_chain")
        orow_t = sem("latent_rows_transposed")
        orow_r = sem("latent_rows_read")
        orow_out = [sem(f"latent_rows_out{j}") for j in range(2)]
        hq_in = sem("head_weights_in")
        proj_done = sem("q_projected")
        proj_hi = sem("head_hi_done")
        qr_t = sem("q_rope_terms")
        qr_lo = sem("q_rope_lo_done")
        s_done = sem("scores_done")
        mx_done = sem("row_max_done")
        rr_done = sem("row_sum_inverted")
        p_done = sem("probabilities_done")
        t_done = sem("prob_transposed")
        pt_hi = sem("prob_hi_done")
        pt_lo = sem("prob_lo_done")
        pv_done = sem("pv_done")
        o_read = sem("pv_read")
        smp_in = sem("sample_tables_in")
        idx_done = sem("page_rows_known")
        wuk_in = sem("w_uk_in")
        wuv_in = sem("w_uv_in")
        c_in_q = [[sem(f"cache{j}_in{g}") for g in range(4)] for j in range(2)]
        k_in = [sem(f"cache_rope{j}_in") for j in range(2)]
        ql_t = sem("w_uk_transposed")
        ql_r = sem("w_uk_read")
        ql_p = sem("q_latent_done")
        ql_c = sem("q_latent_read")
        qc_done = sem("sample_queries_set")
        ct_done = sem("cache_transposed")
        ct_c = sem("cache_latent_read")
        ct_k = sem("cache_rope_read")
        sc_done = sem("sample_scores_done")
        new_done = sem("new_scores_done")
        m1_done = sem("lane_max_done")
        mt_done = sem("lane_max_transposed")
        dg_done = sem("max_diagonal")
        bc_done = sem("max_broadcast")
        sub_done = sem("scores_shifted")
        ex_done = sem("sample_exp_done")
        rs_done = sem("lane_sums_done")
        spv_done = sem("sample_pv_done")
        ol_done = sem("sample_out_done")
        vs_done = sem("sample_v_done")
        vs_read = sem("sample_v_read")
        vh_done = sem("v_hi_done")
        vl_done = sem("v_lo_done")
        gm_in = [sem(f"gate_b_and_merged_a_in{j}") for j in range(2)]
        mg_done = sem("merge_steps")
        mh_done = sem("merged_hi_done")
        ml_done = sem("merged_lo_done")
        xt_in = [sem(f"x_tile_in{j}") for j in range(2)]
        fr_in = sem("ffn_state_in")
        pf_t = sem("ffn_state_transposed")
        pf_r = sem("ffn_state_read")
        l1_s = sem("ln1_sum_steps")
        l1_c = sem("ln1_centred")
        l1_sq = sem("ln1_squared")
        l1_s2 = sem("ln1_squares_added")
        l1_rs = sem("ln1_rstd_done")
        l1_n = sem("ln1_normalised")
        l1_x = sem("ln1_scaled")
        l1_h = sem("ln1_hi_done")
        l1_l = sem("ln1_lo_done")
        l1_a = sem("residual_scaled")
        pad_set = sem("ffn_padding_zeroed")
        se_set = sem("ffn_small_set")
        h_chain = sem("ffn_conv_chain")
        si_done = sem("ffn_silu_done")
        f_done = sem("ffn_inner_done")
        fh_done = sem("ffn_inner_hi_done")
        fl_done = sem("ffn_inner_lo_done")
        dn_done = sem("down_tile_done")
        gb2_in = sem("ln2_rows_in")
        y_t = sem("y_transposed")
        y_st = sem("ln2_stats_steps")
        y_sd = sem("ln2_root_done")
        y_rs = sem("ln2_scale_steps")
        y_n = sem("ln2_normalised")
        y_g = sem("ln2_gain_done")
        y_b = sem("ln2_bias_done")
        y_out = [sem(f"y_out{j}") for j in range(4)]
        kf_t = sem("ffn_rows_transposed")
        kf_r = sem("ffn_rows_read")
        ffn_out = sem("ffn_state_out")

        N1B = 4 * MT
        N1C = N1B + 6
        N2 = N1C + MT
        N3 = N2 + 2 * H
        N4 = N3 + MT
        N5 = N4 + MT

        uses = [5, 4]
        ring = {}

        def take(name, j):
            ring[name] = (j, uses[j])
            uses[j] += 1

        U1A = list(uses)
        uses = [uses[0] + 2 * MT, uses[1] + 2 * MT]
        for k, name in enumerate(("kv0", "kv1", "mean", "kr", "q0", "var", "q1", "q2", "ya0", "ya1",
                                  "skv", "sq", "ya2", "ya3", "ya4", "ya5", "ya6", "ya7")):
            take(name, k % 2)
        U2 = list(uses)
        uses = [uses[0] + 6 * H, uses[1] + 6 * H]
        assert uses == [U2[0] + 6 * H, U2[1] + 6 * H]
        for k in range(MT):
            take(f"mla{k}", k % 2)
        for k in range(MT):
            take(f"mix{k}", k % 2)
        take("mean1", 0)
        take("var1", 1)
        U5 = list(uses)

        GATE0, VAL0, DOWN0, GATE1, VAL1, DOWN1 = range(6)
        NG = FT // 2
        PAIRS = (NG - 1) // 2
        assert NG % 2 == 1

        def kinds(g):
            return (GATE0, VAL0, GATE1, VAL1) if g == "first" else (DOWN0, DOWN1) if g == "last" else range(6)

        def blk(g, kind):
            if g in ("first", "last"):
                n = (N5 if g == "first" else N5 + 4 + 6 * (NG - 1)) + list(kinds(g)).index(kind)
                return n, n
            n = N5 + 4 + kind + 6 * g[1]
            return 12 * g[0] + n, n

        def acc5(g, kind, q, mm=0):
            if g == "first":
                return U5[q] + (kind == GATE1 or kind == VAL1)
            if g == "last":
                return U5[q] + 2 + 6 * (NG - 1) + (2 if kind == DOWN1 else 0) + mm // 2
            k = {GATE0: 0, VAL0: 0, DOWN0: 1, GATE1: 3, VAL1: 3, DOWN1: 4}[kind] + mm // 2
            return 12 * g[0] + (U5[q] + 2 + 6 * g[1] + k)

        def inner(g, kind):
            t = 1 if kind in (GATE1, VAL1) else 0
            return (t if g == "first" else 4 * g[0] + (2 + 2 * g[1] + t)), t

        w_in_v = A["w_in"].rearrange("l (k p) c -> p (l k) c", p=P)
        w_co_v = A["w_conv_out"].rearrange("l (k p) c -> p (l k) c", p=P)

        def slot3(t, n):
            return t[:, n % t.shape[1], :].rearrange("p (k c) -> p k c", c=P)

        def split(x):
            return x.rearrange("p (c n) -> p c n", n=CH)

        gate_cols = (0, D, C_G + D, C_G)
        kr_parts = ((0, 64, 0), (64, 32, 32), (96, 32, 0))

        block = ctx.enter_context(nc.Block())

        @block.sync
        def _(sp):
            for t in range(4):
                sp.dma_start(xrow[t][:, :], A["x_prompt"][0, t * P:(t + 1) * P, :]).then_inc(x_in[t], 16)
                if t == 0:
                    sp.dma_start(ident[:, :], A["c_ident"]).then_inc(c_in, 16)
            for t in range(4, 9):
                sp.wait_ge(x_hi, t - 3)
                if t < 8:
                    sp.dma_start(xrow[t % 4][:, :], A["x_prompt"][0, t * P:(t + 1) * P, :]).then_inc(x_in[t % 4], 16)
                else:
                    sp.dma_start(xrow[0][0:NS, :], A["x_sample"].rearrange("b t c -> (b t) c")).then_inc(x_in[0], 16)
            sp.dma_start(maskc[:, :], A["c_mask"]).then_inc(c2_in, 16)

            def load(n, src):
                sp.wait_ge(lo_done, n + 1)
                sp.dma_start(slot3(wraw, n % RAW), src).then_inc(raw_in[n % RAW], 16)

            load(0, w_in_v[:, :, 0:P])
            load(1, w_in_v[:, :, D:D + P])
            row = lambda v: v.rearrange("l (r p) -> (l r) p", p=P)
            rows = [(0, row(A["b_in"][:, 0:C_KR])), (V_GA, row(A["b_in"][:, C_G:])),
                    (V_CB, row(A["conv_dw_b"])), (V_LG, row(A["conv_ln_g"])), (V_LB, row(A["conv_ln_b"])),
                    (V_QG, row(A["q_norm_g"])), (V_KG, row(A["kv_norm_g"])), (V_FB, row(A["ffn_dw_b"])),
                    (V_L1G, row(A["ln1_g"])), (V_L1B, row(A["ln1_b"]))]
            for r, v in rows:
                sp.dma_start(vrow[r:r + v.shape[0], :], v).then_inc(v_in, 16)
            for c, w, f in kr_parts:
                sp.dma_start(vrow[V_KR:V_KR + 1, c:c + w], A["b_in"][:, C_KR + f:C_KR + f + w]).then_inc(v_in, 16)
            sp.dma_start(crow[0:CW * MT // 2, :, :], A["conv_dw_w"][0].rearrange("k (m p) -> (k m) p", p=P)
                         .rearrange("(h r) p -> r h p", h=2)).then_inc(v_in, 16)
            sp.dma_start(frow[0:FW * FT, :, :], A["ffn_dw_w"][0].rearrange("k (m p) -> (k m) p", p=P)
                         .rearrange("(h r) p -> r h p", h=2)).then_inc(v_in, 16)
            sp.dma_start(strows[:, :, :], A["state_conv"][0].rearrange("(h b) k c -> (b k) h c", h=2)
                         ).then_inc(st_in, 16)

            for t in (2, 3):
                load(t, w_in_v[:, :, gate_cols[t]:gate_cols[t] + P])
            with sp.Fori(1, MT) as m:
                for t in range(4):
                    sp.wait_ge(lo_done, 4 * m + (t + 1))
                    sp.dma_start(slot3(wraw, t % RAW), w_in_v[:, :, bass.ds(m * P + gate_cols[t], P)]
                                 ).then_inc(raw_in[t % RAW], 16)
            n = N1B
            for c in (C_KV, C_KV + P):
                load(n, w_in_v[:, :, c:c + P])
                n += 1
            sp.wait_ge(lo_done, n + 1)
            for c, w, f in kr_parts:
                sp.dma_start(slot3(wraw, n % RAW)[:, :, c:c + w], w_in_v[:, :, C_KR + f:C_KR + f + w]
                             ).then_inc(kr_in if c else raw_in[n % RAW], 16)
            n += 1
            for c in range(3):
                load(n, w_in_v[:, :, C_Q + c * P:C_Q + (c + 1) * P])
                n += 1
            with sp.Fori(0, MT // 2) as i:
                for t in range(2):
                    sp.wait_ge(lo_done, 2 * i + (N1C + t + 1))
                    sp.dma_start(slot3(wraw, (N1C + t) % RAW), w_co_v[:, :, bass.ds(i * (2 * P) + t * P, P)]
                                 ).then_inc(raw_in[(N1C + t) % RAW], 16)
            uq = A["w_uq"][0].rearrange("(k p) c -> p k c", p=P)
            uk = A["w_uk"][0].rearrange("(k p) h n -> p k (h n)", p=P)
            uv = A["w_uv"][0].rearrange("(k p) h n -> p k (h n)", p=P)
            HQ = DN + DR
            with sp.Fori(0, H) as h:
                sp.wait_ge(lo_done, 2 * h + (N2 + 1))
                s0, s1_ = slot3(wraw, N2), slot3(wraw, N2 + 1)
                sp.dma_start(s0[:, 0:3, :], uq[:, :, bass.ds(h * HQ, DN)]).then_inc(raw_in[0], 16)
                for c, w, f in kr_parts:
                    sp.dma_start(s0[:, 3:6, c:c + w], uq[:, :, bass.ds(h * HQ + (DN + f), w)]).then_inc(hq_in, 16)
                sp.dma_start(s0[:, 6:8, :], uk[:, :, bass.ds(h * DN, DN)]).then_inc(hq_in, 16)
                sp.wait_ge(lo_done, 2 * h + (N2 + 2))
                sp.dma_start(s1_[:, 0:2, :], uv[:, :, bass.ds(h * DV, DV)]).then_inc(raw_in[1], 16)

            wv = lambda name: A[name].rearrange("l (k p) c -> p (l k) c", p=P)
            w_mla_v, w_mix_v, w_up_v = wv("w_mla_out"), wv("w_mix_out"), wv("w_up")
            w_dn_v = A["w_down"].rearrange("l (k p) c -> p (l k) c", p=P)

            def w_next(n):
                if n < N4:
                    load(n, w_mla_v[:, :, (n - N3) * P:(n - N3 + 1) * P])
                elif n < N5:
                    load(n, w_mix_v[:, :, (n - N4) * P:(n - N4 + 1) * P])
                else:
                    c = ((n - N5) // 2) * P + ((n - N5) % 2) * F
                    load(n, w_up_v[:, :, c:c + P])

            def merge_in(m):
                sp.dma_start(tmp[m % 2][:, :], gb_d[m]).then_inc(gm_in[m % 2], 16)
                sp.dma_start(stg[m % 2][:, :], ma_d[m]).then_inc(gm_in[m % 2], 16)

            w_next(N3)
            w_next(N3 + 1)
            sp.wait_ge(spv_done, NB + 2)
            sp.wait_ge(ma_out[0], 16 * (MT // 2 + 1))
            sp.wait_ge(ma_out[1], 16 * (MT // 2 + 1))
            for j in range(2):
                sp.wait_ge(stg_out[j], 16 * (MT + 4))
            merge_in(0)
            merge_in(1)
            for m in range(MT):
                w_next(N3 + m + 2)
                sp.wait_ge(mg_done, m + 1)
                if m + 2 < MT:
                    merge_in(m + 2)
                else:
                    sp.dma_start(stg[m % 2][:, :], xt_d[m + 2 - MT]).then_inc(xt_in[m % 2], 16)
            sp.dma_start(frows[:, :], A["state_ffn_conv"][0].rearrange("b t c -> (b t) c")).then_inc(fr_in, 16)
            for m in range(MT):
                w_next(N4 + m + 2)
                if m + 2 < MT:
                    q, n = ring[f"mix{m}"]
                    sp.wait_ge(free[q], n + 2)
                    sp.dma_start(stg[m % 2][:, :], xt_d[m + 2]).then_inc(xt_in[m % 2], 16)

            def ffn_load(g, kind):
                n, ns = blk(g, kind)
                sp.wait_ge(lo_done, n + 1)
                if kind in (DOWN0, DOWN1):
                    cols = slice(0, D // 2) if kind == DOWN0 else slice(D // 2, D)
                    rows_ = slice(FT - 2, FT) if g == "last" else bass.ds(g[0] * 4 + 2 * g[1], 2)
                    dst = wraw[:, ns % RAW, :].rearrange("p (k c) -> p k c", k=2)
                    sp.dma_start(dst, w_dn_v[:, rows_, cols]).then_inc(raw_in[ns % RAW], 16)
                else:
                    t = kind in (GATE1, VAL1)
                    c = (P if t else 0) + (F if kind in (VAL0, VAL1) else 0)
                    cols = slice(c, c + P) if g == "first" else bass.ds(g[0] * (4 * P) + (c + 2 * P * (1 + g[1])), P)
                    sp.dma_start(slot3(wraw, ns), w_up_v[:, :, cols]).then_inc(raw_in[ns % RAW], 16)

            for kind in (GATE1, VAL1):
                ffn_load("first", kind)
            with sp.Fori(0, PAIRS) as i:
                for s in range(2):
                    for kind in range(6):
                        ffn_load((i, s), kind)
            for kind in kinds("last"):
                ffn_load("last", kind)
            sp.wait_ge(h_chain, 12 * FT + 12)
            sp.wait_ge(se_set, 2 * FT)
            sp.dma_start(g2[:, :], A["ln2_g"].to_broadcast([P, D])).then_inc(gb2_in, 16)
            sp.dma_start(b2[:, :], A["ln2_b"].to_broadcast([P, D])).then_inc(gb2_in, 16)

            for t in range(9):
                n = P if t < 8 else NS
                sp.wait_ge(y_b, t + 1)
                dst = O["y_p"][0, t * P:(t + 1) * P, :] if t < 8 else O["y_s"].rearrange("b t c -> (b t) c")
                sp.dma_start(dst, yrow[t % 4][0:n, :]).then_inc(y_out[t % 4], 16)

            sp.dma_start(O["conv_s"][0, :, 0:HALO - NT, :], A["state_conv"][0, :, NT:, :]).then_inc(out_s, 16)

            sp.wait_ge(out_s, 16)
            sp.wait_ge(krow_out, 16 * (NB + 1))
            sp.wait_ge(orow_out[0], 32 * 5)
            sp.wait_ge(orow_out[1], 32 * 4)
            sp.wait_ge(ffn_out, 16 * (1 + NB))
            for j in range(4):
                sp.wait_ge(y_out[j], 16 * (3 if j else 4))

        @block.scalar
        def _(act):
            def hi(n):
                act.wait_ge(raw_in[n % RAW], 16 * (n // RAW + 1))
                act.wait_ge(w_used, n + 1)
                nc.scalar.activation(whi[:, n % HL, :], wraw[:, n % RAW, :], ACT.Copy).then_inc(hi_done, 1)

            for j in range(2):
                act.sem_inc(stg_out[j], 16)
                act.sem_inc(ma_out[j], 16)
            for t in range(9):
                n = P if t < 8 else NS
                act.wait_ge(xt_ready, t + 1)
                nc.scalar.activation(xh[:, :, t * P:t * P + n],
                                     psx[t % 2][:, 0:2, :].rearrange("p b (k n) -> p (b k) n", n=P)[:, :, 0:n],
                                     ACT.Copy).then_inc(x_hi, 1)
            hi(0)
            hi(1)
            act.wait_ge(tr_done, 1)
            nc.scalar.activation(vec[:, 0:V_ROWS], pst[:, 0, 0:V_ROWS], ACT.Copy)
            nc.scalar.activation(cwv[:, :], pst[:, 0, 128:376], ACT.Copy)
            nc.scalar.activation(fwv[:, :], pst[:, 0, 376:508], ACT.Copy).then_inc(tr_read, 1)
            for r in range(4):
                act.wait_ge(tr_done, 2 + r)
                nc.scalar.activation(stT[:, 2 * r:2 * r + 2, :],
                                     pst[:, (r + 1) % 2, 0:480].rearrange("p (m n) -> p m n", m=2),
                                     ACT.Copy).then_inc(tr_read, 1)
            act.wait_ge(c2_in, 16)
            nc.scalar.activation(maskb[:, :], maskc[:, :], ACT.Copy)
            nc.scalar.activation(identb[:, :], ident[:, :], ACT.Copy)
            act.wait_ge(tr_read, 5)

            with act.Fori(0, MT // 2) as i:
                for s in range(2):
                    m = 2 * i + s
                    for t in range(4):
                        act.wait_ge(raw_in[t % RAW], 32 * m + 16 * ((t + 2) // 2 + 1))
                        act.wait_ge(w_used, 4 * m + (t + 3))
                        nc.scalar.activation(whi[:, (t + 2) % HL, :], wraw[:, t % RAW, :], ACT.Copy
                                             ).then_inc(hi_done, 1)
                        if t == 0:
                            act.wait_ge(conv_done, m + 1)
                            act.wait_ge(halo_set, 1)
                            nc.scalar.activation(gs_ext[s][:, :, 0:HALO],
                                                 stT[:, bass.ds(m, 1), :].rearrange("p o (b k) -> p (o b) k", b=NB),
                                                 ACT.Copy)
                            act.wait_ge(w_used, 4 * m + (HL + 1))
                            nc.scalar.activation(split(g_ext[s][:, HALO:]), acc(0), ACT.Identity,
                                                 bias=vec[:, bass.ds(m + V_A, 1)]).then_inc(free[0], 1)
                        elif t == 1:
                            act.wait_ge(w_used, 4 * m + (HL + 2))
                            nc.scalar.activation(split(sg[s][:, :]), acc(1), ACT.Sigmoid,
                                                 bias=vec[:, bass.ds(m + V_GL, 1)]).then_inc(free[1], 1)
                        else:
                            act.wait_ge(w_used, 4 * m + (HL + t + 1))
                            act.wait_ge(stg_out[t % 2], 16 * m + 16)
                            nc.scalar.activation(split(stg[t % 2][:, :]), acc(t), ACT.Sigmoid,
                                                 bias=vec[:, bass.ds(m + (V_GB if t == 2 else V_GA), 1)]
                                                 ).then_inc(free[t % 2], 1)
                            act.wait_ge(free[t % 2], 2 * m + (U1A[t % 2] + 3))
                            act.dma_start((gb_d if t == 2 else ga_d)[bass.ds(m, 1), :, :].rearrange("o p n -> p (o n)"),
                                          stg[t % 2][:, :]).then_inc(stg_out[t % 2], 16)

            def read_z(name, k, j, v):
                hi(N1B + k + 2)
                q, n = ring[name]
                act.wait_ge(w_used, N1B + k + HL + 1)
                act.wait_ge(stg_out[j], 16 * (MT + k // 2 + 1))
                nc.scalar.activation(split(stg[j][:, :]), acc(q), ACT.Identity, bias=vec[:, v:v + 1]
                                     ).then_inc(free[q], 1)
                act.wait_ge(free[q], n + 2)
                act.dma_start(z_d[k], stg[j][:, :]).then_inc(stg_out[j], 16)

            def squares(ms):
                for m in ms:
                    act.wait_ge(ln_c, m + 1)
                    if m >= 2:
                        act.wait_ge(ln_s2, m)
                    nc.scalar.activation(tmp[m % 2][:, :], u[:, m, :], ACT.Square).then_inc(ln_sq, 1)

            def stat_read(name, k, dst, scale, eps=None):
                q, n = ring[name]
                act.wait_ge(stat_done, k)
                if eps is None:
                    nc.scalar.activation(split(dst), acc(q), ACT.Copy, scale=scale).then_inc(free[q], 1)
                else:
                    nc.scalar.activation(split(dst), acc(q), ACT.Sqrt, scale=scale, bias=eps).then_inc(free[q], 1)

            act.wait_ge(kr_in, 32)
            read_z("kv0", 0, 0, V_KV)
            read_z("kv1", 1, 1, V_KV + 1)
            for m in range(MT):
                act.wait_ge(keep_tr, m + 1)
                nc.scalar.activation(krow[0][0:HALO, m * P:(m + 1) * P], pst[0:HALO, m % 2, 0:P], ACT.Copy)
                nc.scalar.activation(krow[1][0:NS, m * P:(m + 1) * P], pst[0:NS, m % 2, P:2 * P], ACT.Copy
                                     ).then_inc(keep_rd, 1)
            act.wait_ge(keep_rd, MT)
            act.dma_start(O["conv_p"][0, 0], krow[0][0:HALO, :]).then_inc(krow_out, 16)
            for b in range(NB):
                act.dma_start(O["conv_s"][0, b, HALO - NT:, :], krow[1][b * NT:(b + 1) * NT, :]).then_inc(krow_out, 16)
            act.wait_ge(krow_out, 16 * (NB + 1))
            stat_read("mean", 1, stat[:, :], 1.0 / D)
            squares(range(0, 4))
            read_z("kr", 2, 0, V_KR)
            squares(range(4, 8))
            read_z("q0", 3, 1, V_Q)
            stat_read("var", 2, s1[:, :], 1.0 / D, LN_EPS)
            read_z("q1", 4, 0, V_Q + 1)
            read_z("q2", 5, 1, V_Q + 2)
            for m in range(MT):
                act.wait_ge(ln_n, m + 1)
                if m >= 2:
                    act.wait_ge(sl_done, m - 1)
                nc.scalar.activation(tmp[m % 2][:, :], u[:, m, :], ACT.Silu, scale=vec[:, V_LG + m:V_LG + m + 1],
                                     bias=vec[:, V_LB + m:V_LB + m + 1]).then_inc(ln_act, 1)
                act.wait_ge(ln_act, m + 1)
                nc.scalar.activation(sh[:, m, :], tmp[m % 2][:, :], ACT.Copy).then_inc(sh_done, 1)

            act.wait_ge(w_used, N1C + HL)
            for j in range(2):
                act.wait_ge(stg_out[j], 16 * (MT + 4))
            act.dma_start(zbuf[:, :, :], z_d.rearrange("k p n -> p k n")).then_inc(z_in, 16)
            for j in range(2):
                act.dma_start(gab[j][:, :], ga_d[j]).then_inc(ga_in[j], 16)
            act.dma_start(cs[:, :], A["c_rope"]).then_inc(cs_in, 16)
            act.wait_ge(z_in, 16)
            for k in range(5):
                nc.scalar.activation(sqb[:, k, :], zbuf[:, k if k < 2 else k + 1, :], ACT.Square).then_inc(rms_sq, 1)

            def after_ya(m):
                if m + 2 < MT:
                    hi(N1C + m + 2)
                q, n = ring[f"ya{m}"]
                act.wait_ge(free[q], n + 2)
                act.dma_start(ma_d[m], stg[m % 2][:, :]).then_inc(ma_out[m % 2], 16)
                if m + 2 < MT:
                    act.dma_start(gab[m % 2][:, :], ga_d[m + 2]).then_inc(ga_in[m % 2], 16)

            def hi_head(h, s):
                act.wait_ge(raw_in[0], 16 * h + 16 * (N2 // RAW + 1))
                act.wait_ge(hq_in, 64 * h + 64)
                act.wait_ge(w_used, 2 * h + (N2 + 1))
                nc.scalar.activation(whi[:, (N2 + 2 * s) % HL, :], wraw[:, 0, :], ACT.Copy).then_inc(hi_done, 1)

            def hi_head_v(h, s):
                act.wait_ge(raw_in[1], 16 * h + 16 * (N2 // RAW + 1))
                act.wait_ge(w_used, 2 * h + (N2 + 2))
                nc.scalar.activation(whi[:, (N2 + 1 + 2 * s) % HL, 0:2 * P], wraw[:, 1, 0:2 * P], ACT.Copy
                                     ).then_inc(hi_done, 1)

            after_ya(0)
            after_ya(1)
            stat_read("skv", 3, rk[:, :], 1.0 / KL, RMS_EPS)
            stat_read("sq", 4, rq[:, :], 1.0 / QL, RMS_EPS)
            after_ya(2)
            after_ya(3)
            act.wait_ge(cs_in, 16)
            for k in range(2):
                act.wait_ge(rms_n, k + 1)
                nc.scalar.activation(ckvh[:, k, :], zbuf[:, k, :], ACT.Copy).then_inc(rms_h, 1)
            after_ya(4)
            act.wait_ge(rms_n, 3)
            nc.scalar.activation(kr2[0:DR, :], zbuf[0:DR, 2, :], ACT.Copy).then_inc(rms_h, 1)
            nc.scalar.activation(kr2[DR:P, :], zbuf[0:DR, 2, :], ACT.Copy).then_inc(rms_h, 1)
            after_ya(5)
            for k in range(3):
                act.wait_ge(rms_n, k + 4)
                nc.scalar.activation(qnh[:, k, :], zbuf[:, k + 3, :], ACT.Copy).then_inc(rms_h, 1)
            after_ya(6)
            hi_head(0, 0)
            hi_head_v(0, 0)
            after_ya(7)
            act.dma_start(mnew[:, :, :], A["c_new"]).then_inc(smp_in, 16)
            act.dma_start(part[:, :], A["c_part"]).then_inc(smp_in, 16)
            act.dma_start(ptb[:, :], A["page_table"]).then_inc(smp_in, 16)
            act.wait_ge(ma_out[0], 16 * 5)
            act.wait_ge(ma_out[1], 16 * 5)
            for t in range(9):
                n = P if t < 8 else NS
                j = t % 2
                act.wait_ge(orow_t, t + 1)
                if t >= 2:
                    act.wait_ge(orow_out[j], 32 * (t // 2))
                if t == 8:
                    nc.scalar.activation(cnr[:, :], pst[0:n, j, 0:KL], ACT.Copy)
                nc.scalar.activation(orow[j][0:n, :], pst[0:n, j, 0:KL + DR], ACT.Copy).then_inc(orow_r, 1)
                act.wait_ge(orow_r, t + 1)
                if t < 8:
                    dc, dk = O["ckv_p"][0, 0, t * P:(t + 1) * P, :], O["kr_p"][0, 0, t * P:(t + 1) * P, :]
                else:
                    dc, dk = (O[x][0].rearrange("b t c -> (b t) c") for x in ("ckv_s", "kr_s"))
                act.dma_start(dc, orow[j][0:n, 0:KL]).then_inc(orow_out[j], 16)
                act.dma_start(dk, orow[j][0:n, KL:]).then_inc(orow_out[j], 16)
            nc.scalar.activation(cnT[:, :, :], zbuf[:, 0:2, S:], ACT.Copy)
            nc.scalar.activation(krT[:, :], zbuf[0:DR, 2, S:], ACT.Copy).then_inc(orow_r, 1)

            def cum(i):
                return i if i < 4 else 4 + 2 * (i - 4)

            def act_project(h, s):
                act.wait_ge(orow_r, 10)
                act.wait_ge(proj_done, 2 * h + 1)
                nc.scalar.activation(split(qh[:, :]), acc(0), ACT.Copy, scale=SCALE).then_inc(proj_hi, 1)
                act.wait_ge(qr_t, 3 * h + 3)
                nc.scalar.activation(qr2[0:DR, :], qrf[0:DR, :], ACT.Copy).then_inc(proj_hi, 1)
                act.wait_ge(w_used, 2 * h + (N2 + HL + 1))
                nc.scalar.activation(knh[:, :].rearrange("p (b n) -> p b n", b=2), psx[0][:, 0:2, :], ACT.Copy
                                     ).then_inc(proj_hi, 1)

            def act_values(h, s):
                act.wait_ge(w_used, 2 * h + (N2 + HL + 2))
                nc.scalar.activation(vh[:, :, :].rearrange("p (b k) n -> p b (k n)", b=2), psx[1][:, 0:2, :], ACT.Copy
                                     ).then_inc(proj_hi, 1)

            def act_head(h, s, more):
                for i in range(10):
                    if i < 8:
                        act.wait_ge(mx_done, 8 * h + (i + 1))
                        act.wait_ge(t_done, 12 * h + (cum(i - 1) + 3 if i >= 2 else 1 + 2 * i))
                        n = (i + 1) * P
                        src = psx[i % 2][:, :, :].rearrange("p b n -> p (b n)")[:, 0:n]
                        nc.scalar.activation(pbuf[i % 2][:, 0:n], src, ACT.Exp, bias=nmx[:, i:i + 1],
                                             accum_out=rs[:, i:i + 1]).then_inc(free[i % 2], 1)
                    if i == 8 and more:
                        act_project(h + 1, 1 - s)
                    if 1 <= i <= 8:
                        q = i - 1
                        for g in range(cum(q + 1) - cum(q)):
                            nb = min(4, q + 1 - 4 * g)
                            act.wait_ge(t_done, 12 * h + (cum(q) + g + 4))
                            act.wait_ge(pv_done, 4 * h + (q // 2 + 1))
                            bank = (cum(q) + g) % 2
                            nc.scalar.activation(pth[:, 4 * g:4 * g + nb, (q % 2) * P:(q % 2 + 1) * P],
                                                 pst[:, bank, 0:nb * P].rearrange("p (k n) -> p k n", n=P), ACT.Copy
                                                 ).then_inc(pt_hi, 1)
                    if i >= 3 and i % 2 == 1:
                        a_ = (i - 3) // 2
                        act.wait_ge(pv_done, 4 * h + (a_ + 2))
                        nc.scalar.activation(vt[:, bass.ds(h, 1), a_ * 2 * P:(a_ + 1) * 2 * P].rearrange("p o n -> p (o n)"),
                                             psx[a_ % 2][:, 2, 0:2 * P], ACT.Copy).then_inc(o_read, 1)
                    if i == 2 and more:
                        hi_head(h + 1, 1 - s)
                        hi_head_v(h + 1, 1 - s)
                if more:
                    act_values(h + 1, 1 - s)

            act.sem_inc(o_read, 2)
            act_project(0, 0)
            act_values(0, 0)
            with act.Fori(0, H // 2 - 1) as i:
                for s in range(2):
                    act_head(2 * i + s, s, True)
            act_head(H - 2, 0, True)
            act_head(H - 1, 1, False)

            act.wait_ge(pv_done, 4 * H + 1)
            act.dma_start(wukp[:, :, :], A["w_uk"][0].rearrange("(k p) h n -> p k (h n)", p=P)).then_inc(wuk_in, 16)
            act.dma_start(wuvp[:, :, :], A["w_uv"][0].rearrange("(k p) h n -> p k (h n)", p=P)).then_inc(wuv_in, 16)
            hi(N3)
            hi(N3 + 1)
            for r in range(4):
                act.wait_ge(ql_t, r + 1)
                nc.scalar.activation(wukT[:, 2 * r:2 * r + 2, :, :].rearrange("p h k n -> p (h k n)"),
                                     pst[:, r % 2, :], ACT.Copy).then_inc(ql_r, 1)

            def act_sample(b, j, first):
                for g in range(8):
                    act.wait_ge(ct_done, 8 * b + (g + 1))
                    act.wait_ge(sc_done, 8 * b + (g + 1))
                    nc.scalar.activation(ct[g % 2][:, 0:8, :].rearrange("p (b k) n -> p b (k n)", b=2),
                                         psx[g % 2][:, 0:2, :], ACT.Copy).then_inc(ct_c, 1)
                    if g == 1 and not first:
                        act_exp(b - 1, 1 - j)

            def act_exp(b, j):
                act.wait_ge(sub_done, 3 * b + 4)
                nc.scalar.activation(px[j][:, :, :], px[j][:, :, :], ACT.Exp).then_inc(ex_done, 1)
                nc.scalar.activation(sn[:, :], sn[:, :], ACT.Exp).then_inc(ex_done, 1)

            act_sample(0, 0, True)
            with act.Fori(0, NB // 2 - 1) as i:
                act_sample(2 * i + 1, 1, False)
                act_sample(2 * i + 2, 0, False)
            act_sample(NB - 1, 1, False)
            act_exp(NB - 1, 1)
            act.wait_ge(vs_done, 1)
            nc.scalar.activation(vt[:, :, S:], pst[:, 0, 0:H * NS].rearrange("p (h n) -> p h n", h=H), ACT.Copy
                                 ).then_inc(vs_read, 1)
            act.wait_ge(vs_read, 1)
            for m in range(MT):
                nc.scalar.activation(vth[:, m, :], vt[:, m, :], ACT.Copy).then_inc(vh_done, 1)
            for m in range(MT):
                hi(N3 + m + 2)
                act.wait_ge(mg_done, m + 1)
                act.wait_ge(vl_done, MT)
                nc.scalar.activation(mgh[:, m, :], mt[m % 2][:, :], ACT.Copy).then_inc(mh_done, 1)
            for m in range(MT):
                hi(N4 + m + 2)
            act.wait_ge(pf_t, 2)
            nc.scalar.activation(pfx[:, 0:32, :, :].rearrange("p f b t -> p (f b t)"), pst[:, 0, :], ACT.Copy
                                 ).then_inc(pf_r, 1)
            nc.scalar.activation(pfx[:, 32:, :, :].rearrange("p f b t -> p (f b t)"), pst[:, 1, 0:(2 * FT - 32) * 16],
                                 ACT.Copy).then_inc(pf_r, 1)
            stat_read("mean1", 5, stat[:, :], 1.0 / D)
            for m in range(MT):
                act.wait_ge(l1_c, m + 1)
                if m >= 2:
                    act.wait_ge(l1_s2, m)
                nc.scalar.activation(tmp[m % 2][:, :], res[:, m, :], ACT.Square).then_inc(l1_sq, 1)
            stat_read("var1", 6, s1[:, :], 1.0 / D, LN_EPS)
            for m in range(MT):
                act.wait_ge(l1_n, m + 1)
                nc.scalar.activation(res[:, m, :], res[:, m, :], ACT.Identity, scale=vec[:, V_L1G + m:V_L1G + m + 1],
                                     bias=vec[:, V_L1B + m:V_L1B + m + 1]).then_inc(l1_x, 1)
                act.wait_ge(l1_x, m + 1)
                nc.scalar.activation(x1h[:, m, :], res[:, m, :], ACT.Copy).then_inc(l1_h, 1)

            def ffn_hi(g, kind):
                order = [(g, k) for k in kinds(g)]
                if g == "first":
                    order += [((0, 0), GATE0), ((0, 0), VAL0)]
                    g2_, k2 = order[list(kinds(g)).index(kind) + 2]
                    n, ns = blk(g2_, k2)
                elif g == "last":
                    return
                else:
                    n, ns = blk(g, kind)
                    n, ns = n + 2, ns + 2
                act.wait_ge(raw_in[ns % RAW], 8 * (n - (ns % RAW)) + 16)
                act.wait_ge(w_used, n + 1)
                nc.scalar.activation(whi[:, ns % HL, :], wraw[:, ns % RAW, :], ACT.Copy).then_inc(hi_done, 1)

            def act_ffn(g):
                for kind in kinds(g):
                    ffn_hi(g, kind)
                    if kind in (DOWN0, DOWN1):
                        continue
                    n, ns = blk(g, kind)
                    q, t = inner(g, kind)
                    v = 1 if kind in (VAL0, VAL1) else 0
                    f = slice(q + v * FT, q + v * FT + 1) if g == "first" else bass.ds(q + v * FT, 1)
                    one = lambda x: x.rearrange("p o n -> p (o n)")
                    if v:
                        act.wait_ge(h_chain, 12 * q + 18)
                        nc.scalar.activation(hb[0][:, :], hb[0][:, :], ACT.Silu).then_inc(si_done, 1)
                    act.wait_ge(h_chain, 12 * q + (12 if v else 6))
                    act.wait_ge(w_used, n + (HL + 1))
                    nc.scalar.activation(split(ue[v][:, FW - 1:]), acc(v), ACT.Copy).then_inc(free[v], 1)
                    nc.scalar.activation(se[v][:, :, 0:FW - 1], pfx[:, f, :, :].rearrange("p o b t -> p (o b) t"), ACT.Copy)
                    act.wait_ge(free[v], acc5(g, kind, v) + 2)
                    new = ue[v][:, FW - 1 + S:].rearrange("p (b t) -> p b t", t=NT)
                    nc.scalar.activation(se[v][:, :, FW - 1:], new, ACT.Copy)
                    nc.scalar.activation(one(kf[:, f, 0:FW - 1]), ue[v][:, S:S + FW - 1], ACT.Copy)
                    nc.scalar.activation(kf[:, f, FW - 1:].rearrange("p o (b t) -> p (o b) t", t=FW - 1),
                                         new[:, :, NT - FW + 1:], ACT.Copy).then_inc(se_set, 1)
                    if v:
                        act.wait_ge(f_done, q + 2)
                        p_ = 0 if g == "first" else (1 + g[1]) % 2
                        nc.scalar.activation(fh[p_][:, t, :], hb[1][:, :], ACT.Copy).then_inc(fh_done, 1)

            act_ffn("first")
            with act.Fori(0, PAIRS) as i:
                for s in range(2):
                    act_ffn((i, s))
            for j in range(4):
                act.sem_inc(y_out[j], 16)
            for r in range(FT // 2):
                act.wait_ge(kf_t, r + 1)
                nc.scalar.activation(fout[:, r * 512:(r + 1) * 512], pst[0:FK, r % 2, :], ACT.Copy).then_inc(kf_r, 1)
            act.wait_ge(kf_r, FT // 2)
            act.dma_start(O["ffn_p"][0, 0], fout[0:FW - 1, :]).then_inc(ffn_out, 16)
            for b in range(NB):
                r = (FW - 1) * (1 + b)
                act.dma_start(O["ffn_s"][0, b], fout[r:r + FW - 1, :]).then_inc(ffn_out, 16)
            for t in range(9):
                n = P if t < 8 else NS
                j = t % 2
                act.wait_ge(y_st, 3 * t + 3)
                nc.scalar.activation(sd[j][0:n, 0:1], mv[j][0:n, 1:2], ACT.Sqrt, bias=LN_EPS).then_inc(y_sd, 1)
                act.wait_ge(y_rs, 2 * t + 2)
                act.wait_ge(y_out[t % 4], 16 * (t // 4 + 1))
                nc.scalar.activation(yrow[t % 4][0:n, :], psx[j][0:n, 0:2, :].rearrange("p b n -> p (b n)"),
                                     ACT.Identity, scale=sd[j][0:n, 1:2], bias=mv[j][0:n, 0:1]).then_inc(y_n, 1)

        @block.gpsimd
        def _(pool):
            pool.sem_inc(lo_done, RAW)
            for t in range(9):
                n = P if t < 8 else NS
                pool.wait_ge(free[t % 2], t // 2 + 2)
                pool.dma_start(xt_d[:, :, t * P:t * P + n].rearrange("m p n -> p m n"), xst[t % 2][:, :, 0:n]
                               ).then_inc(xt_out[t % 2], 16)

            def lo(n):
                pool.wait_ge(hi_done, n + 1)
                nc.gpsimd.tensor_tensor(wlo[:, n % HL, :], wraw[:, n % RAW, :], whi[:, n % HL, :].bitcast(F32),
                                        ALU.subtract).then_inc(lo_done, 1)

            with pool.Fori(0, MT) as m:
                for t in range(4):
                    pool.wait_ge(hi_done, 4 * m + (t + 1))
                    nc.gpsimd.tensor_tensor(wlo[:, t, :], wraw[:, t % RAW, :], whi[:, t, :].bitcast(F32),
                                            ALU.subtract).then_inc(lo_done, 1)
            for n in range(N1B, N1C):
                lo(n)
            for n in range(N1C, N2):
                lo(n)

            with pool.Fori(0, H // 2) as i:
                for s in range(2):
                    for v, w in ((0, D), (1, 2 * P)):
                        n = N2 + 2 * s + v
                        pool.wait_ge(hi_done, 4 * i + (n + 1))
                        nc.gpsimd.tensor_tensor(wlo[:, n % HL, 0:w], wraw[:, v, 0:w],
                                                whi[:, n % HL, 0:w].bitcast(F32), ALU.subtract).then_inc(lo_done, 1)

            kv_rows = A["cache_kv_latent"].rearrange("l g (a r) c -> (l g a) (r c)", r=8)
            kr_rows = A["cache_k_rope"].rearrange("l g (a r) c -> (l g a) (r c)", r=32)

            def gather(b, j):
                pool.indirect_dma_start(kb[j][:, :, :].rearrange("p t c -> p (t c)"), None, kr_rows,
                                        bass.IndirectOffsetOnAxis(ap=idx[:, b, 4:5], axis=0)
                                        ).then_inc(k_in[j], 16)
                for g in range(4):
                    pool.indirect_dma_start(cb[j][:, 8 * g:8 * g + 8, :].rearrange("p t c -> p (t c)"), None, kv_rows,
                                            bass.IndirectOffsetOnAxis(ap=idx[:, b, g:g + 1], axis=0)
                                            ).then_inc(c_in_q[j][g], 16)

            pool.wait_ge(idx_done, 5)
            pool.wait_ge(s_done, 8 * H)
            pool.wait_ge(orow_out[0], 32 * 5)
            pool.wait_ge(orow_out[1], 32 * 4)
            lo(N3)
            lo(N3 + 1)
            gather(0, 0)
            pool.wait_ge(ql_t, 4)
            gather(1, 1)
            for b in range(2, NB):
                pool.wait_ge(spv_done, b + 1)
                gather(b, b % 2)

            for n in range(N3 + 2, N5 + 2):
                lo(n)

            def pool_ffn(g):
                for kind in kinds(g):
                    n, ns = blk(g, kind)
                    pool.wait_ge(hi_done, n + 3)
                    nc.gpsimd.tensor_tensor(wlo[:, (ns + 2) % HL, :], wraw[:, (ns + 2) % RAW, :],
                                            whi[:, (ns + 2) % HL, :].bitcast(F32), ALU.subtract).then_inc(lo_done, 1)

            pool_ffn("first")
            with pool.Fori(0, PAIRS) as i:
                for s in range(2):
                    pool_ffn((i, s))
            pool.wait_ge(gb2_in, 32)
            for t in range(9):
                n = P if t < 8 else NS
                pool.wait_ge(y_g, t + 1)
                nc.gpsimd.tensor_tensor(yrow[t % 4][0:n, :], yrow[t % 4][0:n, :], b2[0:n, :], ALU.add).then_inc(y_b, 1)

        @block.vector
        def _(dve):
            nc.vector.memset(ones[:, :], 1.0).then_inc(ones_set, 1)
            nc.vector.memset(s1[:, :], 0.0)
            dve.sem_inc(free[0], 1)
            dve.sem_inc(free[1], 1)
            dve.sem_inc(conv_done, 2)
            for t in range(9):
                n = P if t < 8 else NS
                src = psx[t % 2][:, 0:2, :].rearrange("p b (k n) -> p (b k) n", n=P)[:, :, 0:n]
                dve.wait_ge(x_hi, t + 1)
                nc.vector.tensor_tensor(xl[:, :, t * P:t * P + n], src, xh[:, :, t * P:t * P + n].bitcast(F32),
                                        ALU.subtract)
                if t >= 2:
                    dve.wait_ge(xt_out[t % 2], 16 * (t // 2))
                nc.vector.tensor_copy(xst[t % 2][:, :, 0:n], src).then_inc(free[t % 2], 1)
            for j in range(2):
                last = nc.vector.memset(g_ext[j][:, 0:HALO], 0.0)
            last.then_inc(halo_set, 1)
            dve.wait_ge(halo_set, 1)
            dve.wait_ge(tr_read, 1)
            dve.wait_ge(xt_out[0], 16 * 5)
            dve.wait_ge(xt_out[1], 16 * 4)

            STEPS = 5 + 2 * CW
            with dve.Fori(0, MT // 2) as i:
                for s in range(2):
                    m = 2 * i + s
                    at_ = [0]

                    def link(ins):
                        ins.then_inc(conv_chain, 1)
                        at_[0] += 1
                        return at_[0]

                    def after(k):
                        dve.wait_ge(conv_chain, STEPS * m + k)

                    link(nc.vector.tensor_copy(wtap[:, s, 0:CW],
                                               cwv[:, :].rearrange("p (k m) -> p m k", m=MT)[:, bass.ds(m, 1), :]
                                               .rearrange("p o k -> p (o k)")))
                    link(nc.vector.tensor_copy(wtap[:, s, CW:CW + 1], vec[:, bass.ds(m + V_CB, 1)]))
                    dve.wait_ge(free[1], 2 * m + (U1A[1] + 2))
                    k = link(nc.vector.tensor_tensor(g_ext[s][:, HALO:], g_ext[s][:, HALO:], sg[s][:, :], ALU.mult))
                    after(k)
                    link(nc.vector.tensor_copy(gs_ext[s][:, :, HALO:],
                                               g_ext[s][:, HALO + S:].rearrange("p (b t) -> p b t", t=NT)))
                    last = link(nc.vector.tensor_copy(keep[:, bass.ds(m, 1), :].rearrange("p o k -> p (o k)"),
                                                      g_ext[s][:, S:]))
                    acc_s = stat[:, S:].rearrange("p (b t) -> p b t", t=NT)
                    um = u[:, bass.ds(m, 1), :].rearrange("p o n -> p (o n)")
                    for k in range(CW):
                        out_p = um[:, 0:S] if k == CW - 1 else stat[:, 0:S]
                        out_s_ = um[:, S:].rearrange("p (b t) -> p b t", t=NT) if k == CW - 1 else acc_s
                        gp, gq = g_ext[s][:, k:k + S], gs_ext[s][:, :, k:k + NT]
                        w = wtap[:, s, k:k + 1]
                        if k == 0:
                            after(last)
                            link(nc.vector.tensor_scalar(out_p, gp, w, wtap[:, s, CW:CW + 1], ALU.mult, ALU.add))
                            last = link(nc.vector.tensor_scalar(out_s_, gq, w, wtap[:, s, CW:CW + 1], ALU.mult, ALU.add))
                        else:
                            after(last - 1)
                            link(nc.vector.scalar_tensor_tensor(out=out_p, in0=gp, scalar=w, in1=stat[:, 0:S],
                                                                op0=ALU.mult, op1=ALU.add))
                            after(last)
                            last = link(nc.vector.scalar_tensor_tensor(out=out_s_, in0=gq, scalar=w, in1=acc_s,
                                                                       op0=ALU.mult, op1=ALU.add))
                    assert at_[0] == STEPS
                    after(last)
                    dve.wait_ge(conv_done, m + 2)
                    nc.vector.tensor_tensor(s1[:, :], s1[:, :], um, ALU.add).then_inc(conv_done, 1)

            def ready(name):
                q, n = ring[name]
                dve.wait_ge(free[q], n + 2)

            dve.wait_ge(stat_done, 1)
            nc.vector.memset(s1[:, :], 0.0).then_inc(ln_s2, 1)
            ready("mean")
            for m in range(MT + 1):
                if m < MT:
                    nc.vector.tensor_tensor(u[:, m, :], u[:, m, :], stat[:, :], ALU.subtract).then_inc(ln_c, 1)
                if m:
                    dve.wait_ge(ln_sq, m)
                    dve.wait_ge(ln_s2, m)
                    nc.vector.tensor_tensor(s1[:, :], s1[:, :], tmp[(m - 1) % 2][:, :], ALU.add).then_inc(ln_s2, 1)
            ready("var")
            nc.vector.reciprocal(stat[:, :], s1[:, :]).then_inc(rstd_done, 1)
            dve.wait_ge(rstd_done, 1)
            for m in range(MT + 1):
                if m < MT:
                    nc.vector.tensor_tensor(u[:, m, :], u[:, m, :], stat[:, :], ALU.mult).then_inc(ln_n, 1)
                if m:
                    dve.wait_ge(sh_done, m)
                    nc.vector.tensor_tensor(sl[:, m - 1, :], tmp[(m - 1) % 2][:, :], sh[:, m - 1, :].bitcast(F32),
                                            ALU.subtract).then_inc(sl_done, 1)

            def merge_a(m):
                q, n = ring[f"ya{m}"]
                dve.wait_ge(w_used, N1C + m + HL + 1)
                dve.wait_ge(ga_in[m % 2], 16 * (m // 2 + 1))
                dve.wait_ge(ma_out[m % 2], 16 * (m // 2 + 1))
                nc.vector.tensor_tensor(split(stg[m % 2][:, :]), acc(q), split(gab[m % 2][:, :]), ALU.mult
                                        ).then_inc(free[q], 1)

            merge_a(0)
            merge_a(1)
            ready("skv")
            nc.vector.reciprocal(rk[:, :], rk[:, :]).then_inc(rms_c, 1)
            merge_a(2)
            ready("sq")
            nc.vector.reciprocal(rq[:, :], rq[:, :]).then_inc(rms_c, 1)
            merge_a(3)
            dve.wait_ge(rms_c, 1)
            for k in range(2):
                nc.vector.scalar_tensor_tensor(out=zbuf[:, k, :], in0=zbuf[:, k, :], scalar=vec[:, V_KG + k:V_KG + k + 1],
                                               in1=rk[:, :], op0=ALU.mult, op1=ALU.mult).then_inc(rms_n, 1)
            dve.wait_ge(cs_in, 16)
            nc.vector.tensor_tensor(qrt2[0:DR, :], zbuf[DR:P, 2, :], cs[DR:P, :], ALU.mult)
            nc.vector.tensor_tensor(zbuf[0:DR, 2, :], zbuf[0:DR, 2, :], cs[0:DR, :], ALU.mult).then_inc(rms_c, 1)
            dve.wait_ge(rms_c, 3)
            nc.vector.tensor_tensor(zbuf[0:DR, 2, :], zbuf[0:DR, 2, :], qrt2[0:DR, :], ALU.add).then_inc(rms_n, 1)
            for k in range(2):
                dve.wait_ge(rms_h, k + 1)
                nc.vector.tensor_tensor(ckvl[:, k, :], zbuf[:, k, :], ckvh[:, k, :].bitcast(F32), ALU.subtract
                                        ).then_inc(rms_l, 1)
            merge_a(4)
            for k in range(3):
                nc.vector.scalar_tensor_tensor(out=zbuf[:, k + 3, :], in0=zbuf[:, k + 3, :],
                                               scalar=vec[:, V_QG + k:V_QG + k + 1], in1=rq[:, :], op0=ALU.mult,
                                               op1=ALU.mult).then_inc(rms_n, 1)
            merge_a(5)
            dve.wait_ge(rms_h, 4)
            nc.vector.tensor_tensor(krl[0:DR, :], zbuf[0:DR, 2, :], kr2[0:DR, :].bitcast(F32), ALU.subtract
                                    ).then_inc(rms_l, 1)
            merge_a(6)
            for k in range(3):
                dve.wait_ge(rms_h, k + 5)
                nc.vector.tensor_tensor(qnl[:, k, :], zbuf[:, k + 3, :], qnh[:, k, :].bitcast(F32), ALU.subtract
                                        ).then_inc(rms_l, 1)
            merge_a(7)

            def cum(i):
                return i if i < 4 else 4 + 2 * (i - 4)

            def dve_project(h, s):
                dve.wait_ge(proj_hi, 4 * h + 1)
                nc.vector.tensor_scalar(qsn[:, bass.ds(h, 1), :].rearrange("p o n -> p (o n)"), psx[0][:, 2, CH - NS:CH],
                                        SCALE, None, ALU.mult)
                nc.vector.scalar_tensor_tensor(out=split(ql[:, :]), in0=acc(0), scalar=SCALE,
                                               in1=split(qh[:, :].bitcast(F32)), op0=ALU.mult, op1=ALU.subtract
                                               ).then_inc(free[0], 1)
                dve.wait_ge(proj_done, 2 * h + 2)
                nc.vector.scalar_tensor_tensor(out=split(qrf[0:DR, :]), in0=psx[1][0:DR, :, 0:CH], scalar=SCALE,
                                               in1=split(cs[0:DR, :]), op0=ALU.mult, op1=ALU.mult).then_inc(qr_t, 1)
                nc.vector.scalar_tensor_tensor(out=split(qrt[0:DR, :]), in0=psx[1][DR:P, :, 0:CH], scalar=SCALE,
                                               in1=split(cs[DR:P, :]), op0=ALU.mult, op1=ALU.mult).then_inc(free[1], 1)
                dve.wait_ge(free[1], 6 * h + (U2[1] + 2))
                nc.vector.tensor_tensor(qrf[0:DR, :], qrf[0:DR, :], qrt[0:DR, :], ALU.add).then_inc(qr_t, 1)
                dve.wait_ge(qr_t, 3 * h + 2)
                for r in (0, DR):
                    last = nc.vector.tensor_copy(qsr[r:r + DR, bass.ds(h, 1), :].rearrange("p o n -> p (o n)"),
                                                 qrf[0:DR, S:])
                last.then_inc(qr_t, 1)
                dve.wait_ge(proj_hi, 4 * h + 2)
                nc.vector.tensor_tensor(qr2[DR:P, :], qrf[0:DR, :], qr2[0:DR, :].bitcast(F32), ALU.subtract
                                        ).then_inc(qr_lo, 1)
                dve.wait_ge(proj_hi, 4 * h + 3)
                nc.vector.tensor_tensor(knl[:, :].rearrange("p (b n) -> p b n", b=2), psx[0][:, 0:2, :],
                                        knh[:, :].bitcast(F32).rearrange("p (b n) -> p b n", b=2), ALU.subtract
                                        ).then_inc(free[0], 1)

            def dve_values(h, s):
                dve.wait_ge(proj_hi, 4 * h + 4)
                nc.vector.tensor_tensor(vl[:, :, :].rearrange("p (b k) n -> p b (k n)", b=2), psx[1][:, 0:2, :],
                                        vh[:, :, :].bitcast(F32).rearrange("p (b k) n -> p b (k n)", b=2),
                                        ALU.subtract).then_inc(free[1], 1)

            def dve_head(h, s, more):
                for i in range(9):
                    if i:
                        q = i - 1
                        dve.wait_ge(free[q % 2], 6 * h + (U2[q % 2] + 2 + q // 2 + 2))
                        nc.vector.reciprocal(rr[:, q:q + 1], rs[:, q:q + 1]).then_inc(rr_done, 1)
                        dve.wait_ge(rr_done, 8 * h + (q + 1))
                        n = (q + 1) * P
                        nc.vector.tensor_scalar(pbuf[q % 2][:, 0:n], pbuf[q % 2][:, 0:n], rr[:, q:q + 1], None,
                                                ALU.mult).then_inc(p_done, 1)
                    if i < 8:
                        dve.wait_ge(s_done, 8 * h + (i + 1))
                        src = psx[i % 2][:, :, :].rearrange("p b n -> p (b n)")[:, 0:(i + 1) * P]
                        nc.vector.reduce_max(nmx[:, i:i + 1], src, axis=AX.X, negate=True).then_inc(mx_done, 1)
                    elif more:
                        dve_project(h + 1, 1 - s)
                    if i:
                        for g in range(cum(q + 1) - cum(q)):
                            nb = min(4, q + 1 - 4 * g)
                            dve.wait_ge(pt_hi, 12 * h + (cum(q) + g + 1))
                            cols = slice((q % 2) * P, (q % 2 + 1) * P)
                            nc.vector.tensor_tensor(ptl[:, 4 * g:4 * g + nb, cols],
                                                    pst[:, (cum(q) + g) % 2, 0:nb * P].rearrange("p (k n) -> p k n", n=P),
                                                    pth[:, 4 * g:4 * g + nb, cols].bitcast(F32), ALU.subtract
                                                    ).then_inc(pt_lo, 1)
                if more:
                    dve_values(h + 1, 1 - s)

            dve.sem_inc(pt_lo, 2)
            dve.wait_ge(orow_r, 10)
            dve_project(0, 0)
            dve_values(0, 0)
            dve.wait_ge(smp_in, 16 * 3)
            for g in range(5):
                nc.vector.tensor_scalar(idx[:, :, g], ptb[:, :], 16.0 if g < 4 else 4.0, part[:, g:g + 1],
                                        ALU.mult, ALU.add).then_inc(idx_done, 1)
            with dve.Fori(0, H // 2 - 1) as i:
                for s in range(2):
                    dve_head(2 * i + s, s, True)
            dve_head(H - 2, 0, True)
            dve_head(H - 1, 1, False)

            dve.wait_ge(pv_done, 4 * H + 1)
            hbt = lambda x: x.rearrange("p (h b t) -> p b h t", h=H, b=NB)
            for r in range(2):
                rows_ = slice(r * DR, (r + 1) * DR)
                nc.vector.memset(qall[rows_, 3 - r, :, :], 0.0)
                nc.vector.tensor_copy(qall[rows_, 2 + r, :, :].rearrange("p b (h t) -> p b h t", h=H),
                                      qsr[rows_, :, :].rearrange("p h n -> p (h n)").rearrange(
                                          "p (h b t) -> p b h t", h=H, b=NB)).then_inc(ql_c, 1)
            dve.wait_ge(ql_p, 1)
            for k in range(2):
                nc.vector.tensor_copy(qall[:, k, :, :].rearrange("p b (h t) -> p b h t", h=H),
                                      hbt(psx[0][:, 0, k * H * NS:(k + 1) * H * NS])).then_inc(ql_c, 1)

            tq = lambda x: x.rearrange("p b n -> p (b n)").rearrange("p (t q) -> p t q", q=HT)
            W = psx[1][:, 2, :]

            def rope_evac(b, g):
                dve.wait_ge(ct_done, 8 * b + (2 * g + 1))
                dve.wait_ge(sc_done, 8 * b + (2 * g + 2))
                nc.vector.tensor_copy(rt[:, :, :], psx[0][:, 2, :].rearrange("p (k n) -> p k n", n=P)).then_inc(ct_k, 1)

            def lane_max(b):
                dve.wait_ge(sc_done, 8 * b + 10)
                nc.vector.reduce_max(m1[:, :], tq(pst[:, :, :]).rearrange("p t q -> p q t"), axis=AX.X).then_inc(m1_done, 1)
                dve.wait_ge(new_done, b + 1)
                nc.vector.tensor_tensor(sn[:, :], W[0:NS, 256:256 + HT],
                                        mnew[:, bass.ds(b, 1), :].rearrange("p o n -> p (o n)"), ALU.add).then_inc(m1_done, 1)
                dve.wait_ge(m1_done, 3 * b + 2)
                nc.vector.tensor_tensor(m1[0:NS, :], m1[0:NS, :], sn[:, :], ALU.max).then_inc(m1_done, 1)

            def shift(b, j):
                dve.wait_ge(mt_done, b + 1)
                nc.vector.reduce_max(mxr[:, :], W[0:HT, 288:416], axis=AX.X).then_inc(dg_done, 1)
                dve.wait_ge(dg_done, 2 * b + 1)
                nc.vector.tensor_scalar(dg[:, :], ident[0:HT, 0:HT], mxr[:, 0:1], None, ALU.mult).then_inc(dg_done, 1)
                dve.wait_ge(bc_done, b + 1)
                nc.vector.tensor_copy(bcs[:, :], W[:, 0:HT]).then_inc(sub_done, 1)
                dve.wait_ge(sub_done, 3 * b + 2)
                dve.wait_ge(spv_done, b + 1)
                nc.vector.tensor_tensor(px[j][:, :, :], tq(pst[:, :, :]),
                                        bcs[:, :].unsqueeze(1).to_broadcast([P, NTL, HT]), ALU.subtract
                                        ).then_inc(sub_done, 1)
                nc.vector.tensor_tensor(sn[:, :], sn[:, :], bcs[0:NS, :], ALU.subtract).then_inc(sub_done, 1)

            def lane_sums(b, j):
                dve.wait_ge(ex_done, 2 * b + 2)
                nc.vector.reduce_sum(rs1[:, :], px[j][:, :, :].rearrange("p t q -> p q t"), axis=AX.X).then_inc(rs_done, 1)
                dve.wait_ge(rs_done, 2 * b + 1)
                nc.vector.tensor_tensor(rs1[0:NS, :], rs1[0:NS, :], sn[:, :], ALU.add).then_inc(rs_done, 1)

            def normalise(b):
                dve.wait_ge(spv_done, b + 3)
                nc.vector.reciprocal(rb[:, :], W[:, 32:32 + HT]).then_inc(ol_done, 1)
                dve.wait_ge(ol_done, 2 * b + 2)
                nc.vector.tensor_tensor(ol[:, :, bass.ds(b, 1), :].rearrange("p k o n -> p k (o n)"),
                                        W[:, 64:64 + 2 * HT].rearrange("p (k n) -> p k n", k=2),
                                        rb[:, :].unsqueeze(1).to_broadcast([P, 2, HT]), ALU.mult).then_inc(ol_done, 1)

            def dve_sample(b, j, first):
                nc.vector.tensor_copy(qcur[j][:, :, :], qall[:, :, bass.ds(b, 1), :].rearrange("p k o n -> p k (o n)")
                                      ).then_inc(qc_done, 1)
                rope_evac(b, 0)
                if not first:
                    shift(b - 1, 1 - j)
                rope_evac(b, 1)
                if not first:
                    lane_sums(b - 1, 1 - j)
                    normalise(b - 1)
                rope_evac(b, 2)
                rope_evac(b, 3)
                lane_max(b)

            dve.sem_inc(sub_done, 1)
            dve.sem_inc(ol_done, 1)
            dve.wait_ge(ql_c, 4)
            dve_sample(0, 0, True)
            with dve.Fori(0, NB // 2 - 1) as i:
                dve_sample(2 * i + 1, 1, False)
                dve_sample(2 * i + 2, 0, False)
            dve_sample(NB - 1, 1, False)
            shift(NB - 1, 1)
            lane_sums(NB - 1, 1)
            normalise(NB - 1)
            for m in range(MT):
                dve.wait_ge(vh_done, m + 1)
                nc.vector.tensor_tensor(vtl[:, m, :], vt[:, m, :], vth[:, m, :].bitcast(F32), ALU.subtract
                                        ).then_inc(vl_done, 1)

            def merged_lo(m):
                dve.wait_ge(mh_done, m + 1)
                nc.vector.tensor_tensor(mgl[:, m, :], mt[m % 2][:, :], mgh[:, m, :].bitcast(F32), ALU.subtract
                                        ).then_inc(ml_done, 1)

            for m in range(MT):
                dve.wait_ge(w_used, N3 + m + HL + 1)
                dve.wait_ge(gm_in[m % 2], 32 * (m // 2 + 1))
                q, n = ring[f"mla{m}"]
                if m >= 2:
                    dve.wait_ge(ml_done, m - 1)
                nc.vector.tensor_tensor(split(mt[m % 2][:, :]), acc(q), split(tmp[m % 2][:, :]), ALU.mult
                                        ).then_inc(free[q], 1)
                dve.wait_ge(free[q], n + 2)
                nc.vector.tensor_tensor(mt[m % 2][:, :], mt[m % 2][:, :], stg[m % 2][:, :], ALU.add).then_inc(mg_done, 1)
                if m:
                    merged_lo(m - 1)
            merged_lo(MT - 1)
            dve.wait_ge(ml_done, MT)
            nc.vector.memset(s1[:, :], 0.0).then_inc(l1_s, 1)
            for m in range(MT):
                q, n = ring[f"mix{m}"]
                dve.wait_ge(w_used, N4 + m + HL + 1)
                dve.wait_ge(xt_in[m % 2], 16 * (m // 2 + 1))
                nc.vector.scalar_tensor_tensor(out=split(res[:, m, :]), in0=split(stg[m % 2][:, :]), scalar=ALPHA,
                                               in1=acc(q), op0=ALU.mult, op1=ALU.add).then_inc(free[q], 1)
                dve.wait_ge(free[q], n + 2)
                dve.wait_ge(l1_s, m + 1)
                nc.vector.tensor_tensor(s1[:, :], s1[:, :], res[:, m, :], ALU.add).then_inc(l1_s, 1)
            dve.wait_ge(stat_done, 5)
            nc.vector.memset(s1[:, :], 0.0).then_inc(l1_s2, 1)
            ready("mean1")
            for m in range(MT + 1):
                if m < MT:
                    nc.vector.tensor_tensor(res[:, m, :], res[:, m, :], stat[:, :], ALU.subtract).then_inc(l1_c, 1)
                if m:
                    dve.wait_ge(l1_sq, m)
                    dve.wait_ge(l1_s2, m)
                    nc.vector.tensor_tensor(s1[:, :], s1[:, :], tmp[(m - 1) % 2][:, :], ALU.add).then_inc(l1_s2, 1)
            ready("var1")
            nc.vector.reciprocal(stat[:, :], s1[:, :]).then_inc(l1_rs, 1)
            dve.wait_ge(l1_rs, 1)
            for m in range(MT + 1):
                if m < MT:
                    nc.vector.tensor_tensor(res[:, m, :], res[:, m, :], stat[:, :], ALU.mult).then_inc(l1_n, 1)
                if m:
                    dve.wait_ge(l1_h, m)
                    nc.vector.tensor_tensor(x1l[:, m - 1, :], res[:, m - 1, :], x1h[:, m - 1, :].bitcast(F32),
                                            ALU.subtract).then_inc(l1_l, 1)
            for m in range(MT):
                nc.vector.tensor_scalar(res[:, m, :], res[:, m, :], ALPHA, None, ALU.mult).then_inc(l1_a, 1)

            def ffn_conv(g, kind):
                q, t = inner(g, kind)
                v = 1 if kind in (VAL0, VAL1) else 0
                f = q + v * FT
                tap = lambda k: fwv[:, f + k * 2 * FT:f + k * 2 * FT + 1] if g == "first" else fwv[:, bass.ds(f + k * 2 * FT, 1)]
                bias = vec[:, V_FB + f:V_FB + f + 1] if g == "first" else vec[:, bass.ds(f + V_FB, 1)]
                dve.wait_ge(free[v], acc5(g, kind, v) + 2)
                dve.wait_ge(fl_done if v else f_done, q + 1)
                h_p = hb[v][:, 0:S]
                h_s = hb[v][:, S:].rearrange("p (b t) -> p b t", t=NT)
                c0 = 12 * q + (12 + 6 * v)
                for part_ in range(2):
                    if part_:
                        dve.wait_ge(se_set, 2 * q + (2 if v else 1))
                    for k in range(FW):
                        h = h_s if part_ else h_p
                        src = se[v][:, :, k:k + NT] if part_ else ue[v][:, k:k + S]
                        if k == 0:
                            nc.vector.tensor_scalar(h, src, tap(0), bias, ALU.mult, ALU.add).then_inc(h_chain, 1)
                        else:
                            dve.wait_ge(h_chain, c0 + 3 * part_ + k)
                            nc.vector.scalar_tensor_tensor(out=h, in0=src, scalar=tap(k), in1=h, op0=ALU.mult,
                                                           op1=ALU.add).then_inc(h_chain, 1)

            def ffn_mult(g, kind):
                q, t = inner(g, kind)
                dve.wait_ge(si_done, q + 1)
                dve.wait_ge(h_chain, 12 * q + 24)
                nc.vector.tensor_tensor(hb[1][:, :], hb[0][:, :], hb[1][:, :], ALU.mult).then_inc(f_done, 1)

            def ffn_lo(g, kind):
                q, t = inner(g, kind)
                p_ = 0 if g == "first" else (1 + g[1]) % 2
                dve.wait_ge(fh_done, q + 1)
                nc.vector.tensor_tensor(fl[p_][:, t, :], hb[1][:, :], fh[p_][:, t, :].bitcast(F32), ALU.subtract
                                        ).then_inc(fl_done, 1)

            def down_add(g, kind, mm):
                n, ns = blk(g, kind)
                j2 = 2 * (NG - 1) if g == "last" else 4 * g[0] + 2 * g[1]
                half_ = 1 if kind == DOWN1 else 0
                if mm < 3:
                    dve.wait_ge(dn_done, 3 * j2 + (3 * half_ + mm + 1))
                else:
                    dve.wait_ge(w_used, n + (HL + 1))
                m = 4 * half_ + mm
                q = mm % 2
                nc.vector.tensor_tensor(split(res[:, m, :]), split(res[:, m, :]), acc(q), ALU.add).then_inc(free[q], 1)

            def dve_ffn(g):
                for kind in kinds(g):
                    if kind in (GATE0, GATE1):
                        ffn_conv(g, kind)
                    elif kind in (VAL0, VAL1):
                        ffn_conv(g, kind)
                        if g == "first":
                            ffn_mult(g, kind)
                            ffn_lo(g, kind)
                    elif g != "last":
                        up = VAL0 if kind == DOWN0 else VAL1
                        down_add(g, kind, 0)
                        ffn_mult(g, up)
                        down_add(g, kind, 1)
                        down_add(g, kind, 2)
                        ffn_lo(g, up)
                        down_add(g, kind, 3)
                    else:
                        for mm in range(4):
                            down_add(g, kind, mm)

            dve.sem_inc(h_chain, 12)
            dve.sem_inc(f_done, 1)
            dve.sem_inc(fl_done, 1)
            dve.wait_ge(l1_a, MT)
            for j in range(2):
                last = nc.vector.memset(ue[j][:, 0:FW - 1], 0.0)
            last.then_inc(pad_set, 1)
            dve.wait_ge(pad_set, 1)
            dve_ffn("first")
            with dve.Fori(0, PAIRS) as i:
                for s in range(2):
                    dve_ffn((i, s))
            dve_ffn("last")

            dve.wait_ge(gb2_in, 32)

            def y_stats(t):
                n, j = (P if t < 8 else NS), t % 2
                dve.wait_ge(y_t, t + 1)
                for c in range(2):
                    nc.vector.bn_stats(bst[j][0:n, c, :], psx[j][0:n, c, :]).then_inc(y_st, 1)
                dve.wait_ge(y_st, 3 * t + 2)
                if t >= 2:
                    dve.wait_ge(y_n, t - 1)
                nc.vector.bn_aggr(mv[j][0:n, :], bst[j][0:n, :, :].rearrange("p c s -> p (c s)")).then_inc(y_st, 1)
                dve.wait_ge(y_sd, t + 1)
                nc.vector.reciprocal(sd[j][0:n, 1:2], sd[j][0:n, 0:1]).then_inc(y_rs, 1)
                dve.wait_ge(y_rs, 2 * t + 1)
                nc.vector.scalar_tensor_tensor(out=mv[j][0:n, 0:1], in0=mv[j][0:n, 0:1], scalar=-1.0,
                                               in1=sd[j][0:n, 1:2], op0=ALU.mult, op1=ALU.mult).then_inc(y_rs, 1)

            def y_gain(t):
                n = P if t < 8 else NS
                dve.wait_ge(y_n, t + 1)
                nc.vector.tensor_tensor(yrow[t % 4][0:n, :], yrow[t % 4][0:n, :], g2[0:n, :], ALU.mult).then_inc(y_g, 1)

            for t in range(9):
                y_stats(t)
                if t:
                    y_gain(t - 1)
            y_gain(8)

        @block.tensor
        def _(pe):
            def product(n, j, hi_x, lo_x, ks=KT, stop_inc=w_used, parts=None):
                wh, wl = slot3(whi, n), slot3(wlo, n)
                out = psx[j]
                for k in range(ks):
                    if parts is not None:
                        pe.wait_ge(parts, k + 1)
                    for w, x in ((wh, hi_x), (wh, lo_x), (wl, hi_x)):
                        for c in range(3):
                            last = nc.tensor.matmul(out[:, c, 0:CH], w[:, k, :], x[:, k, c * CH:(c + 1) * CH],
                                                    start=(k == 0 and x is hi_x and w is wh),
                                                    stop=(k == ks - 1 and w is wl))
                last.then_inc(stop_inc, 1)

            def ready(name):
                q, n = ring[name]
                pe.wait_ge(free[q], n + 1)
                return q

            def column_sums(q, xs):
                for i, x in enumerate(xs):
                    for c in range(3):
                        last = nc.tensor.matmul(psx[q][:, c, 0:CH], ones[:, :], x[:, c * CH:(c + 1) * CH],
                                                start=(i == 0), stop=(i == len(xs) - 1))
                last.then_inc(stat_done, 1)

            pe.sem_inc(w_used, HL)
            pe.wait_ge(c_in, 16)
            for t in range(9):
                n = P if t < 8 else NS
                pe.wait_ge(x_in[t % 4], 16 * (t // 4 + 1))
                pe.wait_ge(free[t % 2], t // 2 + 1)
                dst = psx[t % 2][:, 0:2, :].rearrange("p b (k n) -> p (b k) n", n=P)
                for k in range(MT):
                    last = nc.tensor.transpose(dst[:, k, 0:n], xrow[t % 4][0:n, k * P:(k + 1) * P], ident[0:n, 0:n])
                last.then_inc(xt_ready, 1)
            pe.wait_ge(v_in, 16 * 15)
            nc.tensor.transpose(pst[:, 0, 0:V_ROWS], vrow[0:V_ROWS, :], ident[0:V_ROWS, 0:V_ROWS])
            for h in range(2):
                n = CW * MT // 2
                nc.tensor.transpose(pst[:, 0, 128 + h * n:128 + (h + 1) * n], crow[0:n, h, :], ident[0:n, 0:n])
            for h in range(2):
                n = FW * FT
                last = nc.tensor.transpose(pst[:, 0, 376 + h * n:376 + (h + 1) * n], frow[0:n, h, :], ident[0:n, 0:n])
            last.then_inc(tr_done, 1)
            pe.wait_ge(st_in, 16)
            n = NB * HALO // 2
            for r in range(4):
                if r:
                    pe.wait_ge(tr_read, r)
                for mh in range(4):
                    m, h = 2 * r + mh // 2, mh % 2
                    last = nc.tensor.transpose(pst[:, (r + 1) % 2, mh * n:(mh + 1) * n],
                                               strows[:, h, m * P:(m + 1) * P], ident[0:n, 0:n])
                last.then_inc(tr_done, 1)

            pe.wait_ge(x_hi, 9)
            pe.wait_ge(free[0], 6)
            pe.wait_ge(free[1], 5)
            with pe.Fori(0, MT) as m:
                for t in range(4):
                    pe.wait_ge(lo_done, 4 * m + (RAW + t + 1))
                    pe.wait_ge(free[t % 2], 2 * m + (U1A[t % 2] + t // 2 + 1))
                    product(t, t % 2, xh, xl)

            def weighed(n, name, hi_x, lo_x, parts=None):
                pe.wait_ge(lo_done, n + RAW + 1)
                product(n, ready(name), hi_x, lo_x, parts=parts)

            weighed(N1B, "kv0", xh, xl)
            weighed(N1B + 1, "kv1", xh, xl)
            pe.wait_ge(conv_done, MT + 2)
            column_sums(ready("mean"), [s1])
            for m in range(MT):
                if m >= 2:
                    pe.wait_ge(keep_rd, m - 1)
                nc.tensor.transpose(pst[0:HALO, m % 2, 0:P], keep[:, m, 0:HALO], ident[:, :])
                nc.tensor.transpose(pst[0:NS, m % 2, P:2 * P], keep[:, m, HALO:], ident[:, :]).then_inc(keep_tr, 1)
            weighed(N1B + 2, "kr", xh, xl)
            weighed(N1B + 3, "q0", xh, xl)
            pe.wait_ge(ln_s2, MT + 1)
            column_sums(ready("var"), [s1])
            weighed(N1B + 4, "q1", xh, xl)
            weighed(N1B + 5, "q2", xh, xl)
            pe.wait_ge(sl_done, MT)
            weighed(N1C, "ya0", sh, sl)
            weighed(N1C + 1, "ya1", sh, sl)
            pe.wait_ge(rms_sq, 2)
            column_sums(ready("skv"), [sqb[:, k, :] for k in range(2)])
            pe.wait_ge(rms_sq, 5)
            column_sums(ready("sq"), [sqb[:, k, :] for k in range(2, 5)])
            for m in range(2, MT):
                weighed(N1C + m, f"ya{m}", sh, sl)

            pe.wait_ge(rms_n, 3)
            for t in range(9):
                n = P if t < 8 else NS
                j = t % 2
                if t >= 2:
                    pe.wait_ge(orow_r, t - 1)
                for k in range(2):
                    nc.tensor.transpose(pst[0:n, j, k * P:(k + 1) * P], zbuf[:, k, t * P:t * P + n], ident[:, :])
                nc.tensor.transpose(pst[0:n, j, KL:KL + DR], zbuf[0:DR, 2, t * P:t * P + n], ident[0:DR, 0:DR]
                                    ).then_inc(orow_t, 1)

            def cum(i):
                return i if i < 4 else 4 + 2 * (i - 4)

            def mm3(out, pairs, first=True, last=True):
                steps = [(w, x) for wh, wl, xh_, xl_ in pairs for w, x in ((wh, xh_), (wh, xl_), (wl, xh_))]
                for k, (w, x) in enumerate(steps):
                    r = nc.tensor.matmul(out, w, x, start=first and k == 0, stop=last and k == len(steps) - 1)
                return r

            def pe_project(h, s):
                wh, wl = slot3(whi, N2 + 2 * s), slot3(wlo, N2 + 2 * s)
                pe.wait_ge(lo_done, 2 * h + (N2 + RAW + 1))
                for q in range(2):
                    pe.wait_ge(free[q], 6 * h + (U2[q] + 1))
                    if q == 0:
                        pe.wait_ge(o_read, 4 * h + 1)
                    for c in range(3):
                        cols = slice(c * CH, (c + 1) * CH)
                        last = mm3(psx[q][:, c, 0:CH], [(wh[:, 3 * q + k, :], wl[:, 3 * q + k, :], qnh[:, k, cols],
                                                         qnl[:, k, cols]) for k in range(3)])
                    last.then_inc(proj_done, 1)
                pe.wait_ge(free[0], 6 * h + (U2[0] + 2))
                for c in range(2):
                    cols = slice(c * 512, (c + 1) * 512)
                    last = mm3(psx[0][:, c, :], [(wh[:, 6 + k, :], wl[:, 6 + k, :], ckvh[:, k, cols], ckvl[:, k, cols])
                                                 for k in range(2)])
                last.then_inc(w_used, 1)

            def pe_values(h, s):
                wh, wl = slot3(whi, N2 + 1 + 2 * s), slot3(wlo, N2 + 1 + 2 * s)
                pe.wait_ge(lo_done, 2 * h + (N2 + RAW + 2))
                pe.wait_ge(free[1], 6 * h + (U2[1] + 2))
                for t in range(8):
                    cols = slice(t * P, (t + 1) * P)
                    last = mm3(psx[1][:, t // 4, (t % 4) * P:(t % 4 + 1) * P],
                               [(ckvh[:, k, cols], ckvl[:, k, cols], wh[:, k, :], wl[:, k, :]) for k in range(2)])
                last.then_inc(w_used, 1)

            def pe_head(h, s, more):
                for i in range(10):
                    if i < 8:
                        q = i % 2
                        pe.wait_ge(free[q], 6 * h + (U2[q] + 2 + i // 2 + 1))
                        if i == 0:
                            pe.wait_ge(free[0], 6 * h + (U2[0] + 3))
                            pe.wait_ge(qr_lo, h + 1)
                        cols = slice(i * P, (i + 1) * P)
                        for c in range(i // 4 + 1):
                            n = min(512, (i + 1) * P - c * 512)
                            ks = slice(c * 512, c * 512 + n)
                            out = psx[q][:, c, 0:n]
                            mm3(out, [(qh[:, cols], ql[:, cols], knh[:, ks], knl[:, ks])], last=False)
                            nc.tensor.matmul(out, qr2[:, cols], kr2[:, ks], start=False, stop=False)
                            diag = c == i // 4
                            last = nc.tensor.matmul(out, qr2[0:DR, cols], krl[0:DR, ks], start=False, stop=not diag)
                            if diag:
                                last = nc.tensor.matmul(psx[q][:, c, n - P:n], identb[:, :], maskb[:, :],
                                                        start=False, stop=True)
                        last.then_inc(s_done, 1)
                    if i >= 3 and i % 2 == 1:
                        a_ = (i - 3) // 2
                        if i == 9 and more:
                            pe_project(h + 1, 1 - s)
                            pe.wait_ge(free[1], 6 * h + (U2[1] + 8))
                        pe.wait_ge(pt_lo, 12 * h + (cum(2 * a_ + 2) + 2))
                        pe.wait_ge(o_read, 4 * h + (a_ + 1))
                        if a_ == 0:
                            pe.wait_ge(free[1], 6 * h + (U2[1] + 3))
                        k_last = 2 * a_ + 1
                        for k in range(k_last + 1):
                            c0 = P if k == k_last else 0
                            last = mm3(psx[a_ % 2][:, 2, c0:2 * P], [(vh[:, k, :], vl[:, k, :], pth[:, k, c0:],
                                                                      ptl[:, k, c0:])], first=k == 0, last=k == k_last)
                        last.then_inc(pv_done, 1)
                    if 1 <= i <= 8:
                        q = i - 1
                        pe.wait_ge(p_done, 8 * h + (q + 1))
                        for g in range(cum(q + 1) - cum(q)):
                            pe.wait_ge(pt_lo, 12 * h + (cum(q) + g + 1))
                            for k in range(4 * g, min(4 * g + 4, q + 1)):
                                last = nc.tensor.transpose(pst[:, (cum(q) + g) % 2, (k % 4) * P:(k % 4 + 1) * P],
                                                           pbuf[q % 2][:, k * P:(k + 1) * P], ident[:, :])
                            last.then_inc(t_done, 1)
                if more:
                    pe_values(h + 1, 1 - s)

            pe.wait_ge(rms_l, 6)
            pe.wait_ge(orow_r, 9)
            pe.sem_inc(t_done, 3)
            pe.sem_inc(pv_done, 1)
            pe_project(0, 0)
            pe_values(0, 0)
            with pe.Fori(0, H // 2 - 1) as i:
                for s in range(2):
                    pe_head(2 * i + s, s, True)
            pe_head(H - 2, 0, True)
            pe_head(H - 1, 1, False)

            pe.sem_inc(sc_done, 2)
            pe.sem_inc(spv_done, 2)
            pe.wait_ge(wuk_in, 16)
            pe.wait_ge(pt_lo, 12 * H + 2)
            for r in range(4):
                if r >= 2:
                    pe.wait_ge(ql_r, r - 1)
                for v in range(4):
                    h, k = 2 * r + v // 2, v % 2
                    last = nc.tensor.transpose(pst[:, r % 2, v * P:(v + 1) * P], wukp[:, k, h * DN:(h + 1) * DN], ident[:, :])
                last.then_inc(ql_t, 1)
            pe.wait_ge(ql_r, 4)
            pe.wait_ge(free[0], U2[0] + 6 * H + 1)
            pe.wait_ge(free[1], U2[1] + 6 * H + 1)
            pe.wait_ge(o_read, 4 * H + 2)
            for k in range(2):
                for h in range(H):
                    last = nc.tensor.matmul(psx[0][:, 0, (k * H + h) * NS:(k * H + h + 1) * NS], wukT[:, h, k, :],
                                            qsn[:, h, :], start=True, stop=True)
            last.then_inc(ql_p, 1)
            pe.wait_ge(ql_c, 4)

            W = psx[1][:, 2, :]

            def turn(b, j, g):
                if g % 2 == 0:
                    pe.wait_ge(c_in_q[j][g // 2], (b // 2) * 16 + 16 if isinstance(b, int) else half(b, j) * 16 + 16)
                if g == 0:
                    pe.wait_ge(k_in[j], (b // 2) * 16 + 16 if isinstance(b, int) else half(b, j) * 16 + 16)
                dst = psx[g % 2]
                for v in range(4 if g % 2 == 0 else 0):
                    nc.tensor.transpose(psx[0][:, 2, v * P:(v + 1) * P],
                                        kb[j][:, 4 * g + 2 * v:4 * g + 2 * v + 2, :].rearrange("p t c -> p (t c)"),
                                        ident[:, :])
                for v in range(4):
                    for k in range(2):
                        last = nc.tensor.transpose(dst[:, k, v * P:(v + 1) * P],
                                                   cb[j][:, 4 * g + v, k * P:(k + 1) * P], ident[:, :])
                last.then_inc(ct_done, 1)

            def scores(b, j, g):
                pe.wait_ge(ct_c, 8 * b + (g + 1))
                pe.wait_ge(ct_k, 4 * b + (g // 2 + 1))
                if g == 0:
                    pe.wait_ge(qc_done, b + 1)
                for v in range(4):
                    t = 4 * g + v
                    out = pst[:, t // 16, (t % 16) * HT:(t % 16 + 1) * HT]
                    for k in range(2):
                        nc.tensor.matmul(out, ct[g % 2][:, 4 * k + v, :], qcur[j][:, k, :],
                                         start=k == 0, stop=False)
                    last = nc.tensor.matmul(out, rt[:, 2 * (g % 2) + v // 2, :], qcur[j][:, 2 + v % 2, :],
                                            start=False, stop=True)
                last.then_inc(sc_done, 1)

            def new_scores(b, j):
                pe.wait_ge(ol_done, 2 * b + 1)
                out = W[0:NS, 256:256 + HT]
                for k in range(2):
                    nc.tensor.matmul(out, cnT[:, k, :], qcur[j][:, k, :], start=k == 0, stop=False)
                nc.tensor.matmul(out, krT[:, :], qcur[j][0:DR, 2, :], start=False, stop=True
                                 ).then_inc(new_done, 1)

            def maxima(b):
                pe.wait_ge(m1_done, 3 * b + 3)
                nc.tensor.transpose(W[0:HT, 288:416], m1[:, :], ident[:, :]).then_inc(mt_done, 1)
                pe.wait_ge(dg_done, 2 * b + 2)
                nc.tensor.matmul(W[:, 0:HT], ones[0:HT, :], dg[:, :], start=True, stop=True).then_inc(bc_done, 1)

            def values(b, j):
                pe.wait_ge(rs_done, 2 * b + 2)
                nc.tensor.matmul(W[:, 32:32 + HT], ones[:, :], rs1[:, :], start=True, stop=True)
                for k in range(2):
                    out = W[:, 64 + k * HT:64 + (k + 1) * HT]
                    for t in range(NTL):
                        nc.tensor.matmul(out, cb[j][:, t, k * P:(k + 1) * P], px[j][:, t, :], start=t == 0, stop=False)
                    last = nc.tensor.matmul(out, cnr[:, k * P:(k + 1) * P], sn[:, :], start=False, stop=True)
                last.then_inc(spv_done, 1)

            def pe_sample(b, j, first):
                turn(b, j, 0)
                turn(b, j, 1)
                if not first:
                    maxima(b - 1)
                    pe.wait_ge(sub_done, 3 * (b - 1) + 3)
                for g in range(8):
                    scores(b, j, g)
                    if g + 2 < 8:
                        turn(b, j, g + 2)
                    if g == 1 and not first:
                        values(b - 1, 1 - j)
                new_scores(b, j)

            half_of = {}

            def half(b, j):
                return half_of[j]

            pe_sample(0, 0, True)
            with pe.Fori(0, NB // 2 - 1) as i:
                half_of[1], half_of[0] = i, i + 1
                pe_sample(2 * i + 1, 1, False)
                pe_sample(2 * i + 2, 0, False)
            pe_sample(NB - 1, 1, False)
            maxima(NB - 1)
            values(NB - 1, 1)
            pe.wait_ge(wuv_in, 16)
            pe.wait_ge(ol_done, 2 * NB + 1)
            pe.wait_ge(sub_done, 3 * NB + 1)
            for h in range(H):
                for k in range(2):
                    last = nc.tensor.matmul(pst[:, 0, h * NS:(h + 1) * NS], wuvp[:, k, h * DV:(h + 1) * DV],
                                            ol[:, k, :, h * NT:(h + 1) * NT], start=k == 0, stop=k == 1)
            last.then_inc(vs_done, 1)
            for m in range(MT):
                weighed(N3 + m, f"mla{m}", vth, vtl, vl_done if m == 0 else None)
            for m in range(MT):
                weighed(N4 + m, f"mix{m}", mgh, mgl, ml_done if m == 0 else None)
            pe.wait_ge(vs_read, 1)
            pe.wait_ge(fr_in, 16)
            for r in range(2):
                lo_, hi_ = 32 * r, min(2 * FT, 32 * (r + 1))
                for f in range(lo_, hi_):
                    n = NB * (FW - 1)
                    last = nc.tensor.transpose(pst[:, r, (f - lo_) * n:(f - lo_ + 1) * n], frows[:, f * P:(f + 1) * P],
                                               ident[0:n, 0:n])
                last.then_inc(pf_t, 1)
            pe.wait_ge(l1_s, MT + 1)
            column_sums(ready("mean1"), [s1])
            pe.wait_ge(l1_s2, MT + 1)
            column_sums(ready("var1"), [s1])

            def up(g, kind, parts=None):
                n, ns = blk(g, kind)
                v = 1 if kind in (VAL0, VAL1) else 0
                pe.wait_ge(lo_done, n + (RAW + 1))
                pe.wait_ge(free[v], acc5(g, kind, v) + 1)
                product(ns, v, x1h, x1l, parts=parts)

            def down(g, kind):
                n, ns = blk(g, kind)
                wh, wl = (x[:, ns % HL, :].rearrange("p (k c) -> p k c", k=2) for x in (whi, wlo))
                p_ = 0 if g == "last" else g[1]
                j2 = 2 * (NG - 1) if g == "last" else 4 * g[0] + 2 * g[1]
                pe.wait_ge(lo_done, n + (RAW + 1))
                for mm in range(4):
                    q = mm % 2
                    pe.wait_ge(free[q], acc5(g, kind, q, mm) + 1)
                    cols = slice(mm * P, (mm + 1) * P)
                    for k in range(2):
                        if mm == 0 and kind == DOWN0:
                            pe.wait_ge(fl_done, j2 + (k + 2))
                        for w, x in ((wh, fh[p_]), (wh, fl[p_]), (wl, fh[p_])):
                            for c in range(3):
                                last = nc.tensor.matmul(psx[q][:, c, 0:CH], w[:, k, cols], x[:, k, c * CH:(c + 1) * CH],
                                                        start=k == 0 and w is wh and x is fh[p_],
                                                        stop=k == 1 and w is wl)
                    last.then_inc(dn_done if mm < 3 else w_used, 1)

            def pe_ffn(g):
                for kind in kinds(g):
                    if kind in (DOWN0, DOWN1):
                        down(g, kind)
                    else:
                        up(g, kind, l1_l if g == "first" and kind == GATE0 else None)

            pe_ffn("first")
            with pe.Fori(0, PAIRS) as i:
                for s in range(2):
                    pe_ffn((i, s))
            pe_ffn("last")

            pe.wait_ge(se_set, 2 * FT)
            pe.wait_ge(pf_r, 2)
            for r in range(FT // 2):
                if r >= 2:
                    pe.wait_ge(kf_r, r - 1)
                for v in range(4):
                    last = nc.tensor.transpose(pst[0:FK, r % 2, v * P:(v + 1) * P], kf[:, 4 * r + v, :], ident[:, :])
                last.then_inc(kf_t, 1)
            for q in range(2):
                pe.wait_ge(free[q], U5[q] + 2 + 6 * (NG - 1) + 4 + 1)
            for t in range(9):
                n, j = (P if t < 8 else NS), t % 2
                if t >= 2:
                    pe.wait_ge(y_n, t - 1)
                for m in range(MT):
                    last = nc.tensor.transpose(psx[j][0:n, m // 4, (m % 4) * P:(m % 4 + 1) * P],
                                               res[:, m, t * P:t * P + n], ident[:, :])
                last.then_inc(y_t, 1)


_INS = ["x_prompt", "x_sample", "cache_kv_latent", "cache_k_rope", "state_conv", "state_ffn_conv", "page_table",
        "w_in", "b_in", "conv_dw_w", "conv_dw_b", "conv_ln_g", "conv_ln_b", "w_conv_out", "q_norm_g", "w_uq",
        "kv_norm_g", "w_uk", "w_uv", "w_mla_out", "w_mix_out", "ln1_g", "ln1_b", "w_up", "ffn_dw_w", "ffn_dw_b",
        "w_down", "ln2_g", "ln2_b"]
_OUTS = [("y_p", (1, S, D)), ("y_s", (NB, NT, D)), ("ckv_p", (1, 1, S, KL)), ("kr_p", (1, 1, S, DR)),
         ("conv_p", (1, 1, CW - 1, D)), ("ffn_p", (1, 1, FW - 1, 2 * F)), ("ckv_s", (1, NB, NT, KL)),
         ("kr_s", (1, NB, NT, DR)), ("conv_s", (1, NB, CW - 1, D)), ("ffn_s", (1, NB, FW - 1, 2 * F))]


def constants():
    inv = (np.float32(1.0) / np.power(np.float32(10000.0), np.arange(0, DR, 2, dtype=np.float32) / np.float32(DR)))
    pos = np.concatenate([np.arange(S), np.tile(PAST + np.arange(NT), NB)]).astype(np.float32)
    ang = (pos[None, :] * inv.astype(np.float32)[:, None]).astype(np.float64)
    cos, sin = np.cos(ang).astype(np.float32), np.sin(ang).astype(np.float32)
    rope = np.concatenate([cos, cos, -sin, sin], 0)
    mask = np.where(np.arange(P)[None, :] > np.arange(P)[:, None], NEG, 0.0).astype(np.float32)
    new = np.full((NS, NB, H, NT), NEG, np.float32)
    for b in range(NB):
        for t in range(NT):
            new[b * NT:b * NT + t + 1, b, :, t] = 0.0
    a = np.arange(P)[:, None] % 4
    part = np.concatenate([4 * a + np.arange(4)[None, :], a], 1)
    return {"c_ident": np.eye(P, dtype=np.float32), "c_mask": mask, "c_rope": rope,
            "c_new": new.reshape(NS, NB, H * NT), "c_part": part.astype(np.float32)}


def kernel(**inputs):
    import concourse.bacc as _bacc
    from concourse.bass_utils import run_bass_kernel_spmd as _run

    nc = _bacc.Bacc("TRN2", target_bir_lowering=False, num_devices=1)
    arrays, ins, outs = {}, {}, {}
    for name, a in [(n, inputs[n]) for n in _INS] + list(constants().items()):
        if name == "page_table":
            a = np.repeat(np.asarray(a).T, 4, axis=0)
        a = np.ascontiguousarray(a)
        arrays[f"in_{name}"] = a
        ins[name] = nc.dram_tensor(f"in_{name}", a.shape, mybir.dt.from_np(a.dtype), kind="ExternalInput").ap()
    for name, shape in _OUTS:
        outs[name] = nc.dram_tensor(f"out_{name}", shape, F32, kind="ExternalOutput").ap()
    program(nc, ins, outs)
    r = _run(nc, [arrays], core_ids=[0])
    return tuple(r.results[0][f"out_{name}"] for name, _ in _OUTS)
```
